# Optimizing a Trainium2 kernel written in Bass

```python
import math
import jax, jax.numpy as jnp
from jax import lax
import numpy as np

D_MODEL = 1024
BATCH = 1
SEQ = 512
DEPTH = 2
DEC_BATCH = 8
DEC_SEQ = 8
PAST_LEN = 1024
PAGE_SIZE = 128

CONV_W = 4
RMS_EPS = 1e-6
L2_EPS = 1e-6
N_BRANCH = 3
D_RNN = D_MODEL // 2
LRU_BLOCKS = 8
LRU_BS = D_RNN // LRU_BLOCKS
LRU_C = 8.0
NSA_HEADS = 8
NSA_HD = 64
NSA_KV = 2
NSA_REP = NSA_HEADS // NSA_KV
NSA_WIDTH = NSA_HEADS * NSA_HD
CMP_BLOCK = 32
SLC_BLOCK = 64
N_SEL = 16
WINDOW = 512
Q_BLOCK = 128
ROT_DIM = NSA_HD // 4
ROPE_THETA = 500000.0
DN_HEADS = 4
DN_HD = 128
DN_WIDTH = DN_HEADS * DN_HD
DN_CHUNK = 64

SPLIT_SIZES = (D_RNN, D_RNN, NSA_WIDTH, 2 * N_BRANCH * NSA_KV * NSA_HD, NSA_WIDTH, N_BRANCH * NSA_HEADS,
               3 * DN_WIDTH, DN_WIDTH, DN_HEADS, DN_HEADS, N_BRANCH * D_MODEL)
IN_COLS = (2 * D_RNN + 2 * NSA_WIDTH + 2 * N_BRANCH * NSA_KV * NSA_HD + N_BRANCH * NSA_HEADS
           + 4 * DN_WIDTH + 2 * DN_HEADS + N_BRANCH * D_MODEL)

kernel_name = 'hybrid_rglru_nsa_gdn_step'

def rmsnorm(x, g):
    xf = x.astype(jnp.float32)
    y = xf * lax.rsqrt(jnp.mean(xf * xf, axis=-1, keepdims=True) + RMS_EPS)
    return y * g.astype(jnp.float32)

def l2norm(x):
    return x * lax.rsqrt(jnp.sum(x * x, axis=-1, keepdims=True) + L2_EPS)

def masked_softmax(s, mask):
    s = jnp.where(mask, s.astype(jnp.float32), -1e30)
    p = jax.nn.softmax(s, axis=-1)
    return jnp.where(mask, p, 0.0)

def rope(x, pos):
    half = ROT_DIM // 2
    inv = ROPE_THETA ** (-jnp.arange(half, dtype=jnp.float32) * 2.0 / ROT_DIM)
    ang = pos.astype(jnp.float32)[:, None] * inv[None, :]
    shape = (1, pos.shape[0]) + (1,) * (x.ndim - 3) + (half,)
    c = jnp.cos(ang).reshape(shape)
    s = jnp.sin(ang).reshape(shape)
    xf = x.astype(jnp.float32)
    x1, x2, rest = xf[..., :half], xf[..., half:ROT_DIM], xf[..., ROT_DIM:]
    return jnp.concatenate([x1 * c - x2 * s, x2 * c + x1 * s, rest], axis=-1)

def causal_conv(x, buf, w, b=None):
    T = x.shape[1]
    ext = jnp.concatenate([buf.astype(x.dtype), x], axis=1)
    y = ext[:, 0:T] * w[0]
    for j in range(1, CONV_W):
        y = y + ext[:, j:j + T] * w[j]
    if b is not None:
        y = y + b
    return y, ext[:, -(CONV_W - 1):]

def rg_lru(u, h0, wa, ba, wx, bx, lam):
    f32 = jnp.float32
    B, T, _ = u.shape
    uf = u.astype(f32)
    ub = uf.reshape(B, T, LRU_BLOCKS, LRU_BS)
    r = jax.nn.sigmoid(jnp.einsum('btnc,ncd->btnd', ub, wa.astype(f32)).reshape(B, T, D_RNN) + ba)
    i = jax.nn.sigmoid(jnp.einsum('btnc,ncd->btnd', ub, wx.astype(f32)).reshape(B, T, D_RNN) + bx)
    log_a = LRU_C * r * jax.nn.log_sigmoid(lam.astype(f32))
    a = jnp.exp(log_a)
    b = jnp.sqrt(-jnp.expm1(2.0 * log_a)) * (i * uf)
    b = b.at[:, 0].add(a[:, 0] * h0.astype(f32))

    def combine(left, right):
        a_l, b_l = left
        a_r, b_r = right
        return a_l * a_r, a_r * b_l + b_r

    _, hs = lax.associative_scan(combine, (a, b), axis=1)
    return hs, hs[:, -1]

def nsa_cmp_slc(q, q_pos, kc_blk, vc_blk, ks_t, vs_t, n_top):
    B, Tq = q.shape[:2]
    ncb = kc_blk.shape[1]
    nsb = ks_t.shape[2] // SLC_BLOCK
    s = jnp.einsum('bqgrd,bngd->bqgrn', q, kc_blk)
    cmp_ok = (jnp.arange(ncb) * CMP_BLOCK + CMP_BLOCK - 1)[None, :] <= q_pos[:, None]
    p = masked_softmax(s, cmp_ok[None, :, None, None, :])
    o_cmp = jnp.einsum('bqgrn,bngd->bqgrd', p, vc_blk)
    imp = p.sum(axis=3).reshape(B, Tq, NSA_KV, nsb, SLC_BLOCK // CMP_BLOCK).sum(-1)
    blk = jnp.arange(nsb)[None, :]
    cur = (q_pos // SLC_BLOCK)[:, None]
    forced = ((blk == 0) | (blk == cur))[None, :, None, :]
    future = (blk > cur)[None, :, None, :]
    imp = jnp.where(forced, jnp.inf, jnp.where(future, -jnp.inf, imp))
    _, sel = lax.top_k(imp, n_top)
    n_sel_tok = n_top * SLC_BLOCK
    tok = (sel[..., None] * SLC_BLOCK + jnp.arange(SLC_BLOCK)).reshape(B, Tq, NSA_KV, n_sel_tok)
    idx = jnp.transpose(tok, (0, 2, 1, 3)).reshape(B, NSA_KV, Tq * n_sel_tok)
    bi = jnp.arange(B)[:, None, None]
    gi = jnp.arange(NSA_KV)[None, :, None]
    kg = ks_t[bi, gi, idx].reshape(B, NSA_KV, Tq, n_sel_tok, NSA_HD)
    vg = vs_t[bi, gi, idx].reshape(B, NSA_KV, Tq, n_sel_tok, NSA_HD)
    s = jnp.einsum('bqgrd,bgqsd->bqgrs', q, kg)
    ok = (tok <= q_pos[None, :, None, None])[:, :, :, None, :]
    p = masked_softmax(s, ok)
    o_slc = jnp.einsum('bqgrs,bgqsd->bqgrd', p, vg)
    return o_cmp, o_slc

def window_attn(q, k, v, n_prev):
    f32 = jnp.float32
    B, Tq = q.shape[:2]
    qb = Q_BLOCK if Tq % Q_BLOCK == 0 else Tq
    nqb = Tq // qb
    nback = -(-WINDOW // qb)
    front = nback * qb - n_prev
    kw_len = (nback + 1) * qb
    pad = ((0, 0), (front, 0), (0, 0), (0, 0))
    kb = jnp.pad(k, pad).reshape(B, nback + nqb, qb, NSA_KV, NSA_HD)
    vb = jnp.pad(v, pad).reshape(B, nback + nqb, qb, NSA_KV, NSA_HD)
    band = jnp.arange(nqb)[:, None] + jnp.arange(nback + 1)[None, :]
    kw = kb[:, band].reshape(B, nqb, kw_len, NSA_KV, NSA_HD).astype(f32)
    vw = vb[:, band].reshape(B, nqb, kw_len, NSA_KV, NSA_HD).astype(f32)
    qq = q.reshape(B, nqb, qb, NSA_KV, NSA_REP, NSA_HD)
    s = jnp.einsum('bnqgrd,bnkgd->bnqgrk', qq, kw)
    kidx = jnp.arange(nqb)[:, None, None] * qb + jnp.arange(kw_len)[None, None, :]
    qidx = nback * qb + jnp.arange(nqb)[:, None, None] * qb + jnp.arange(qb)[None, :, None]
    ok = (kidx >= front) & (kidx <= qidx) & (qidx - kidx < WINDOW)
    p = masked_softmax(s, ok[None, :, :, None, None, :])
    o = jnp.einsum('bnqgrk,bnkgd->bnqgrd', p, vw)
    return o.reshape(B, Tq, NSA_KV, NSA_REP, NSA_HD)

def gated_delta(q, k, v, g, beta, S0):
    B, T = q.shape[:2]
    C = DN_CHUNK
    Tp = -(-T // C) * C
    nc = Tp // C

    def chunks(a):
        a = jnp.pad(a, ((0, 0), (0, Tp - T)) + ((0, 0),) * (a.ndim - 2))
        a = a.reshape((B, nc, C) + a.shape[2:])
        return jnp.transpose(a, (1, 0, 3, 2) + tuple(range(4, a.ndim)))

    qc, kc, vc = chunks(q), chunks(k), chunks(v)
    gc, bc = chunks(g), chunks(beta)
    G = jnp.cumsum(gc, axis=-1)
    incl = jnp.tril(jnp.ones((C, C), dtype=bool))
    strict = jnp.tril(jnp.ones((C, C), dtype=bool), -1)
    dmat = jnp.exp(jnp.where(incl, G[..., :, None] - G[..., None, :], -jnp.inf))
    kk = jnp.einsum('nbhcd,nbhed->nbhce', kc, kc)
    A = jnp.where(strict, bc[..., :, None] * kk * dmat, 0.0) + jnp.eye(C, dtype=kk.dtype)
    u = lax.linalg.triangular_solve(A, bc[..., None] * vc, left_side=True, lower=True, unit_diagonal=True)
    w = lax.linalg.triangular_solve(A, bc[..., None] * kc * jnp.exp(G)[..., None],
                                    left_side=True, lower=True, unit_diagonal=True)
    qk = jnp.einsum('nbhcd,nbhed->nbhce', qc, kc) * dmat
    qdec = qc * jnp.exp(G)[..., None]
    kdec = kc * jnp.exp(G[..., -1:] - G)[..., None]
    glast = jnp.exp(G[..., -1])

    def step(S, xs):
        u_, w_, qk_, qdec_, kdec_, gl_ = xs
        vn = u_ - jnp.einsum('bhcd,bhde->bhce', w_, S)
        o = jnp.einsum('bhcd,bhde->bhce', qdec_, S) + jnp.einsum('bhce,bhef->bhcf', qk_, vn)
        S = gl_[..., None, None] * S + jnp.einsum('bhcd,bhce->bhde', kdec_, vn)
        return S, o

    S, o = lax.scan(step, S0, (u, w, qk, qdec, kdec, glast))
    o = jnp.transpose(o, (1, 0, 3, 2, 4)).reshape(B, Tp, DN_HEADS, DN_HD)[:, :T]
    return o, S

def hybrid_layer(x, past_kv, win_prev, lru_h0, lru_buf, dn_S0, dn_buf,
                 norm_g, w_in, lru_conv_w, lru_conv_b, lru_wa, lru_ba, lru_wx, lru_bx, lru_lam,
                 q_norm, k_norm, dn_conv_w, dn_A_log, dn_dt_bias, dn_o_norm,
                 w_lru_out, w_nsa_out, w_dn_out, w_out):
    f32 = jnp.float32
    B, T, _ = x.shape
    P = past_kv.shape[1]
    n_prev = win_prev.shape[1]
    pos = P + jnp.arange(T, dtype=jnp.int32)
    h = rmsnorm(x, norm_g).astype(x.dtype)
    proj = h @ w_in
    points = [int(c) for c in np.cumsum(SPLIT_SIZES)[:-1]]
    (lru_x, lru_z, nsa_q, nsa_kv, nsa_z, nsa_g,
     dn_qkv, dn_z, dn_a, dn_b, merge_g) = jnp.split(proj, points, axis=-1)

    u, lru_buf_new = causal_conv(lru_x, lru_buf, lru_conv_w, lru_conv_b)
    lru_seq, lru_h = rg_lru(u, lru_h0, lru_wa, lru_ba, lru_wx, lru_bx, lru_lam)
    out_lru = (lru_seq.astype(x.dtype) * jax.nn.silu(lru_z)) @ w_lru_out

    q = rope(rmsnorm(nsa_q.reshape(B, T, NSA_HEADS, NSA_HD), q_norm), pos) * (NSA_HD ** -0.5)
    qg = q.reshape(B, T, NSA_KV, NSA_REP, NSA_HD)
    kv = nsa_kv.reshape(B, T, 2 * N_BRANCH, NSA_KV, NSA_HD)
    k = rope(rmsnorm(kv[:, :, 0::2], k_norm[:, None, :]), pos).astype(x.dtype)
    v = kv[:, :, 1::2]
    rows = jnp.stack([k[:, :, 0], v[:, :, 0], k[:, :, 1], v[:, :, 1]], axis=2)
    win_rows = jnp.stack([k[:, :, 2], v[:, :, 2]], axis=2)
    full = jnp.concatenate([past_kv.astype(rows.dtype), rows], axis=1)
    L = P + T
    Lp = -(-L // SLC_BLOCK) * SLC_BLOCK
    full = jnp.pad(full, ((0, 0), (0, Lp - L), (0, 0), (0, 0), (0, 0)))
    kc_blk = full[:, :, 0].reshape(B, Lp // CMP_BLOCK, CMP_BLOCK, NSA_KV, NSA_HD).astype(f32).mean(2)
    vc_blk = full[:, :, 1].reshape(B, Lp // CMP_BLOCK, CMP_BLOCK, NSA_KV, NSA_HD).astype(f32).mean(2)
    ks_t = jnp.transpose(full[:, :, 2], (0, 2, 1, 3))
    vs_t = jnp.transpose(full[:, :, 3], (0, 2, 1, 3))
    n_top = min(N_SEL, Lp // SLC_BLOCK)
    qb = Q_BLOCK if T % Q_BLOCK == 0 else T
    nqb = T // qb
    q_blocks = jnp.swapaxes(qg.reshape(B, nqb, qb, NSA_KV, NSA_REP, NSA_HD), 0, 1)
    p_blocks = pos.reshape(nqb, qb)
    o_cmp, o_slc = lax.map(
        lambda a: nsa_cmp_slc(a[0], a[1], kc_blk, vc_blk, ks_t, vs_t, n_top), (q_blocks, p_blocks))
    o_cmp = jnp.swapaxes(o_cmp, 0, 1).reshape(B, T, NSA_KV, NSA_REP, NSA_HD)
    o_slc = jnp.swapaxes(o_slc, 0, 1).reshape(B, T, NSA_KV, NSA_REP, NSA_HD)
    win_all = jnp.concatenate([win_prev.astype(win_rows.dtype), win_rows], axis=1)
    o_win = window_attn(qg, win_all[:, :, 0], win_all[:, :, 1], n_prev)
    bg = jax.nn.sigmoid(nsa_g.astype(f32)).reshape(B, T, N_BRANCH, NSA_KV, NSA_REP)[..., None]
    o_nsa = (bg[:, :, 0] * o_cmp + bg[:, :, 1] * o_slc + bg[:, :, 2] * o_win).reshape(B, T, NSA_WIDTH)
    out_nsa = (o_nsa.astype(x.dtype) * jax.nn.silu(nsa_z)) @ w_nsa_out
    win_state = win_all[:, -min(WINDOW, n_prev + T):]

    qkv, dn_buf_new = causal_conv(dn_qkv, dn_buf, dn_conv_w)
    qkv = jax.nn.silu(qkv.astype(f32))
    dq, dk, dv = jnp.split(qkv, 3, axis=-1)
    dq = l2norm(dq.reshape(B, T, DN_HEADS, DN_HD)) * (DN_HD ** -0.5)
    dk = l2norm(dk.reshape(B, T, DN_HEADS, DN_HD))
    dv = dv.reshape(B, T, DN_HEADS, DN_HD)
    beta = jax.nn.sigmoid(dn_b.astype(f32))
    g = -jnp.exp(dn_A_log.astype(f32)) * jax.nn.softplus(dn_a.astype(f32) + dn_dt_bias.astype(f32))
    o_dn, dn_S = gated_delta(dq, dk, dv, g, beta, dn_S0.astype(f32))
    o_dn = rmsnorm(o_dn, dn_o_norm).reshape(B, T, DN_WIDTH)
    out_dn = (o_dn.astype(x.dtype) * jax.nn.silu(dn_z)) @ w_dn_out

    mg = jax.nn.sigmoid(merge_g.astype(f32)).reshape(B, T, N_BRANCH, D_MODEL)
    merged = mg[:, :, 0] * out_lru + mg[:, :, 1] * out_nsa + mg[:, :, 2] * out_dn
    y = merged.astype(x.dtype) @ w_out
    return x + y.astype(x.dtype), (rows, win_state, lru_h, lru_buf_new, dn_S, dn_buf_new)

def setup_inputs(seed: int = 0) -> dict:
    key = jax.random.key(seed)
    ks = jax.random.split(key, 32)
    f32 = jnp.float32
    n_pages = PAST_LEN // PAGE_SIZE
    n_used = DEC_BATCH * n_pages
    n_phys = n_used + max(1, n_used // 4)
    win_buf = min(WINDOW, PAST_LEN)

    def nrm(k, shape, scale):
        return scale * jax.random.normal(k, shape, f32)

    x_prompt = nrm(ks[0], (BATCH, SEQ, D_MODEL), 1.0)
    x_sample = nrm(ks[1], (DEC_BATCH, DEC_SEQ, D_MODEL), 1.0)
    cache_nsa_kv = nrm(ks[2], (DEPTH, n_phys, PAGE_SIZE, 4, NSA_KV, NSA_HD), 1.0)
    perm = jax.random.permutation(ks[3], n_phys).astype(jnp.int32)
    page_table = perm[:n_used].reshape(DEC_BATCH, n_pages)
    state_nsa_win = nrm(ks[4], (DEPTH, DEC_BATCH, win_buf, 2, NSA_KV, NSA_HD), 1.0)
    state_lru_h = nrm(ks[5], (DEPTH, DEC_BATCH, D_RNN), 0.5)
    state_lru_conv = nrm(ks[6], (DEPTH, DEC_BATCH, CONV_W - 1, D_RNN), 1.0)
    state_dn_S = nrm(ks[7], (DEPTH, DEC_BATCH, DN_HEADS, DN_HD, DN_HD), 0.1)
    state_dn_conv = nrm(ks[8], (DEPTH, DEC_BATCH, CONV_W - 1, 3 * DN_WIDTH), 1.0)

    norm_gain = 1.0 + nrm(ks[9], (DEPTH, D_MODEL), 0.02)
    w_in = nrm(ks[10], (DEPTH, D_MODEL, IN_COLS), D_MODEL ** -0.5)
    lru_conv_w = nrm(ks[11], (DEPTH, CONV_W, D_RNN), CONV_W ** -0.5)
    lru_conv_b = nrm(ks[12], (DEPTH, D_RNN), 0.01)
    lru_wa = nrm(ks[13], (DEPTH, LRU_BLOCKS, LRU_BS, LRU_BS), LRU_BS ** -0.5)
    lru_ba = nrm(ks[14], (DEPTH, D_RNN), 0.01)
    lru_wx = nrm(ks[15], (DEPTH, LRU_BLOCKS, LRU_BS, LRU_BS), LRU_BS ** -0.5)
    lru_bx = nrm(ks[16], (DEPTH, D_RNN), 0.01)
    a_c = jax.random.uniform(ks[17], (DEPTH, D_RNN), f32, 0.9, 0.999)
    a0 = a_c ** (1.0 / LRU_C)
    lru_lambda = jnp.log(a0) - jnp.log1p(-a0)
    nsa_q_norm = 1.0 + nrm(ks[18], (DEPTH, NSA_HD), 0.02)
    nsa_k_norm = 1.0 + nrm(ks[19], (DEPTH, N_BRANCH, NSA_HD), 0.02)
    dn_conv_w = nrm(ks[20], (DEPTH, CONV_W, 3 * DN_WIDTH), CONV_W ** -0.5)
    dn_A_log = jnp.log(jax.random.uniform(ks[21], (DEPTH, DN_HEADS), f32, 1.0, 16.0))
    dt = jnp.exp(jax.random.uniform(ks[22], (DEPTH, DN_HEADS), f32, math.log(1e-3), math.log(1e-1)))
    dn_dt_bias = dt + jnp.log(-jnp.expm1(-dt))
    dn_o_norm = 1.0 + nrm(ks[23], (DEPTH, DN_HD), 0.02)
    w_lru_out = nrm(ks[24], (DEPTH, D_RNN, D_MODEL), D_RNN ** -0.5)
    w_nsa_out = nrm(ks[25], (DEPTH, NSA_WIDTH, D_MODEL), NSA_WIDTH ** -0.5)
    w_dn_out = nrm(ks[26], (DEPTH, DN_WIDTH, D_MODEL), DN_WIDTH ** -0.5)
    w_out = nrm(ks[27], (DEPTH, D_MODEL, D_MODEL), D_MODEL ** -0.5)
    return {
        'x_prompt': x_prompt, 'x_sample': x_sample,
        'cache_nsa_kv': cache_nsa_kv, 'page_table': page_table,
        'state_nsa_win': state_nsa_win, 'state_lru_h': state_lru_h, 'state_lru_conv': state_lru_conv,
        'state_dn_S': state_dn_S, 'state_dn_conv': state_dn_conv,
        'norm_gain': norm_gain, 'w_in': w_in,
        'lru_conv_w': lru_conv_w, 'lru_conv_b': lru_conv_b, 'lru_wa': lru_wa, 'lru_ba': lru_ba,
        'lru_wx': lru_wx, 'lru_bx': lru_bx, 'lru_lambda': lru_lambda,
        'nsa_q_norm': nsa_q_norm, 'nsa_k_norm': nsa_k_norm,
        'dn_conv_w': dn_conv_w, 'dn_A_log': dn_A_log, 'dn_dt_bias': dn_dt_bias, 'dn_o_norm': dn_o_norm,
        'w_lru_out': w_lru_out, 'w_nsa_out': w_nsa_out, 'w_dn_out': w_dn_out, 'w_out': w_out,
    }

def reference(x_prompt, x_sample, cache_nsa_kv, page_table, state_nsa_win, state_lru_h, state_lru_conv,
              state_dn_S, state_dn_conv, norm_gain, w_in, lru_conv_w, lru_conv_b, lru_wa, lru_ba,
              lru_wx, lru_bx, lru_lambda, nsa_q_norm, nsa_k_norm, dn_conv_w, dn_A_log, dn_dt_bias,
              dn_o_norm, w_lru_out, w_nsa_out, w_dn_out, w_out):
    Bp = x_prompt.shape[0]
    Bd = x_sample.shape[0]
    past_len = page_table.shape[1] * PAGE_SIZE
    dt = x_prompt.dtype
    p_kv0 = jnp.zeros((Bp, 0, 4, NSA_KV, NSA_HD), dt)
    p_win0 = jnp.zeros((Bp, 0, 2, NSA_KV, NSA_HD), dt)
    p_h0 = jnp.zeros((Bp, D_RNN), jnp.float32)
    p_lbuf0 = jnp.zeros((Bp, CONV_W - 1, D_RNN), dt)
    p_S0 = jnp.zeros((Bp, DN_HEADS, DN_HD, DN_HD), jnp.float32)
    p_dbuf0 = jnp.zeros((Bp, CONV_W - 1, 3 * DN_WIDTH), dt)
    weights = (norm_gain, w_in, lru_conv_w, lru_conv_b, lru_wa, lru_ba, lru_wx, lru_bx, lru_lambda,
               nsa_q_norm, nsa_k_norm, dn_conv_w, dn_A_log, dn_dt_bias, dn_o_norm,
               w_lru_out, w_nsa_out, w_dn_out, w_out)
    xp, xs = x_prompt, x_sample
    st_p, st_s = [], []
    for l in range(DEPTH):
        lw = [w[l] for w in weights]
        xp, sp = hybrid_layer(xp, p_kv0, p_win0, p_h0, p_lbuf0, p_S0, p_dbuf0, *lw)
        past = cache_nsa_kv[l][page_table].reshape(Bd, past_len, 4, NSA_KV, NSA_HD)
        xs, ss = hybrid_layer(xs, past, state_nsa_win[l], state_lru_h[l], state_lru_conv[l],
                              state_dn_S[l], state_dn_conv[l], *lw)
        st_p.append(sp)
        st_s.append(ss)
    kv_p, win_p, lh_p, lc_p, S_p, dc_p = [jnp.stack(a) for a in zip(*st_p)]
    kv_s, win_s, lh_s, lc_s, S_s, dc_s = [jnp.stack(a) for a in zip(*st_s)]
    return (xp, xs, kv_p, kv_s, win_p, win_s, lh_p, lh_s, lc_p, lc_s, S_p, S_s, dc_p, dc_s)


_drawn_inputs = setup_inputs


def setup_inputs(seed=0):
    import zlib

    import numpy as np

    out = dict(_drawn_inputs(seed))
    spreads = {}
    factors = {'cache_nsa_kv': 3.98,
     'lru_ba': 27.728,
     'lru_bx': 8.0,
     'nsa_q_norm': 8.0,
     'nsa_k_norm': 11.351,
     'dn_o_norm': 6.318}
    for name, (base, spread) in spreads.items():
        noise = np.random.default_rng([zlib.crc32(name.encode()), seed]).standard_normal(out[name].shape)
        drawn = base * np.exp(spread * noise) if base else spread * noise
        out[name] = __import__('jax').numpy.asarray(drawn.astype(out[name].dtype))
    for name, factor in factors.items():
        out[name] = (out[name] * factor).astype(out[name].dtype)
    return out
```

```python
from contextlib import ExitStack

import numpy as np

import concourse.bass as bass
from concourse import mybir

F32 = mybir.dt.float32
I32 = mybir.dt.int32
ALU = mybir.AluOpType
ACT = mybir.ActivationFunctionType
AX = mybir.AxisListType

P = 128
D_MODEL, SEQ, DEPTH, DEC_BATCH, DEC_SEQ = 1024, 512, 2, 8, 8
PAST_LEN, PAGE, N_PHYS = 1024, 128, 80
CONV_W, D_RNN, LRU_BLOCKS, LRU_BS = 4, 512, 8, 64
HEADS, HD, KV, REP = 8, 64, 2, 4
CMP, SLC, WINDOW = 32, 64, 512
DN_H, DN_D, DN_W, CHUNK = 4, 128, 512, 64
NBR = 3
ROT, THETA = 16, 500000.0
RMS_EPS = L2_EPS = 1e-6
NEG = -1e30

T_S = DEC_BATCH * DEC_SEQ
T = SEQ + T_S
HALF = T // 2
KT_M = D_MODEL // P
TILES = [(t, min(P, T - t)) for t in range(0, T, P)]
NTILE = len(TILES)
PAGES = PAST_LEN // PAGE
NPB = PAST_LEN // CMP
NCB = SEQ // CMP
NSEL = PAST_LEN // SLC
HIST = CONV_W - 1
S_EXT = HIST + DEC_SEQ
EXT = HIST + SEQ + DEC_BATCH * S_EXT

SIZES = (D_RNN, D_RNN, HEADS * HD, 6 * KV * HD, HEADS * HD, NBR * HEADS, 3 * DN_W, DN_W, DN_H, DN_H, NBR * D_MODEL)
(C_LX, C_LZ, C_Q, C_KV, C_NZ, C_NG, C_DQKV, C_DZ, C_DA, C_DB, C_MG) = (sum(SIZES[:i]) for i in range(len(SIZES)))
NG = NBR * HEADS
NSM = NG + 2 * DN_H

GW = 256
GT = GW // P


def layout(parts):
    at, n = {}, 0
    for name, size in parts:
        at[name] = (n, size)
        n += size
    return at, n


PAR, NPAR = layout([("gain", 8), ("lconv", 16), ("lcb", 4), ("ba", 4), ("bx", 4), ("lam", 4), ("dconv", 48),
                    ("qn", 1), ("kn", 3), ("on", 1)])

CON, NCON = layout([
    ("ident", P), ("ones", P), ("blk", P), ("swap", P), ("cos", T), ("sin", T),
    ("poolz", NPB + 4 * (PAGES - 1)), ("poolp", 4 * P), ("hmask", HEADS),
    ("U", P), ("R", P), ("SU", P), ("Us", P), ("Rs", P), ("SUs", P), ("lev", 6 * P),
    ("causal", P), ("cmask", 4 * NCB), ("cvalid", 4), ("rsum", P), ("sel", 4 * P), ("gmask", NG),
    ("newm", 4 * T_S), ("winm", DEC_SEQ), ("bmask", DEC_BATCH), ("blkno", NSEL), ("eps", 1),
])


def constants():
    c = {}
    p = np.arange(P)
    row, col = p[:, None], p[None, :]
    c["ident"] = row == col
    c["ones"] = np.ones((P, P))
    c["blk"] = row // HD == col // HD
    half = ROT // 2
    d = col % HD
    c["swap"] = ((row == col - half) & (d >= half) & (d < ROT)) * 1.0 - ((row == col + half) & (d < half)) * 1.0
    pos = np.concatenate([np.arange(SEQ), np.tile(PAST_LEN + np.arange(DEC_SEQ), DEC_BATCH)]).astype(np.float32)
    inv = np.float32(THETA) ** (-np.arange(half, dtype=np.float32) * np.float32(2.0) / np.float32(ROT))
    ang = (pos[None, :] * inv[p % half][:, None].astype(np.float32)).astype(np.float32)
    rot = (row % HD) < ROT
    c["cos"] = np.where(rot, np.cos(ang), 1.0)
    c["sin"] = np.where(rot, np.sin(ang), 0.0)
    z = np.arange(NPB + 4 * (PAGES - 1))[None, :]
    c["poolz"] = (z == 4 * (PAGES - 1) + row // CMP) / CMP
    c["poolp"] = np.concatenate([(col % NCB == 4 * t + row // CMP) / CMP for t in range(4)], 1)
    c["hmask"] = np.arange(HEADS)[None, :] == row // NCB
    for n, q in (("", CHUNK), ("s", DEC_SEQ)):
        same = row // q == col // q
        c["U" + n], c["R" + n], c["SU" + n] = same & (row <= col), same & (row > col), same & (row < col)
    c["lev"] = np.concatenate([(row // (2 * s) == col // (2 * s)) & (col % (2 * s) < s) & (row % (2 * s) >= s)
                               for s in (1, 2, 4, 8, 16, 32)], 1)
    c["causal"] = np.where(col <= row, 0.0, NEG)
    blk = np.arange(NCB)[None, :]
    c["cmask"] = np.concatenate([np.where(blk * CMP + CMP - 1 <= row + t * P, 0.0, NEG) for t in range(4)], 1)
    c["cvalid"] = (row + np.arange(4)[None, :] * P) >= CMP - 1
    b2, g, r, t = p // 64, p // 32 % 2, p // 8 % 4, p % 8
    key = b2 * 100 + g * 10 + t
    c["rsum"] = key[:, None] == key[None, :]
    c["sel"] = np.concatenate([row == ((2 * k + b2) * 8 + t)[None, :] for k in range(4)], 1)
    c["gmask"] = (np.arange(NG)[None, :] % HEADS) == (g * REP + r)[:, None]
    new = np.arange(T_S)[None, :]
    c["newm"] = np.concatenate([np.where((new // 8 == (2 * k + b2)[:, None]) & (new % 8 <= t[:, None]), 0.0, NEG)
                                for k in range(4)], 1)
    c["winm"] = np.where(np.arange(DEC_SEQ)[None, :] > t[:, None], 0.0, NEG)
    c["bmask"] = np.arange(DEC_BATCH)[None, :] == row // DEC_SEQ
    c["blkno"] = np.broadcast_to(np.arange(1, NSEL + 1)[None, :], (P, NSEL))
    c["eps"] = np.full((P, 1), RMS_EPS)
    out = np.zeros((P, NCON), np.float32)
    for name, (at, n) in CON.items():
        out[:, at:at + n] = c[name].astype(np.float32)
    return out


A_NSA, _ = layout([("q", 4 * T), ("k", 3 * T), ("v", 3 * T + 64), ("ktok", NTILE * 6 * P), ("qb", DEC_BATCH * 64),
                   ("s", 1088 + 576), ("kt", PAST_LEN), ("kw", WINDOW), ("cache", 2 * PAGES * 4 * P),
                   ("win", 2 * 4 * 2 * P)])
L0 = A_NSA["qb"][0]
A_LRU, _ = layout([("", L0), ("ext", 4 * EXT), ("u", 4 * T), ("a", 4 * T), ("b", 4 * T), ("t", 4 * T), ("h", 4 * T)])
GRP = 2
A_DN, NDN = layout([("ext", 12 * EXT), ("c", 12 * T), ("qk", GRP * DN_W), ("kd", GRP * DN_W), ("u", GRP * DN_W),
                       ("w", GRP * DN_W), ("S", DN_W), ("S0", 32 * P)])
A_TMP, NTMP = layout([("X", 2 * DN_W), ("Y", 2 * DN_W), ("B", 2 * DN_W), ("W", 2 * DN_W), ("E", 2 * DN_W),
                      ("kb", 2 * DN_W), ("bv", 2 * DN_W)])
A_Z, NZ = layout([("gT", T), ("vcb", HEADS * HD), ("ckv", 2 * 2 * P), ("cpT", P), ("orow", P), ("cp", NPB), ("kcT", NPB),
                  ("ex", NSEL), ("eq", NSEL), ("gsel", 4 * NG)])
A_MG, _ = layout([("m", 8 * T), ("ow", 6 * 4 * GW), ("sg", 2 * T), ("pr", T)])
assert NTMP <= 12 * EXT and NZ <= 4 * T
NARENA = max(NDN, A_NSA["win"][0] + A_NSA["win"][1], A_LRU["h"][0] + A_LRU["h"][1])

DN_GROUPS = [(0, 1), (2, 3), (4,)]

PROJ = ([("lx", c, "V") for c in range(4)] + [("lz", c, "A") for c in range(4)]
        + [("q", c, "V") for c in range(4)] + [("kv", c, "A") for c in range(6)] + [("nz", c, "A") for c in range(4)]
        + [("sm", 0, "V")]
        + [("dc", c, "AV"[c % 2]) for c in range(12)] + [("dz", c, "A") for c in range(4)]
        + [("mg", c, "A") for c in range(24)] + [("wo", c, "V") for c in range(8)])
NP_LRU, NP_NSA, NP_DN = 8, 8 + 15, 8 + 15 + 16
NP_MG = NP_DN + 24
LRU_AT = 14
WIDE = [i for i, (k, _, _) in enumerate(PROJ) if k != "sm"]
RING = 3


def taken(n, who):
    return sum(1 for _, _, w in PROJ[:n] if w == who)


def first_col(kind, c):
    return {"lx": C_LX, "lz": C_LZ, "dc": C_DQKV, "dz": C_DZ, "kv": C_KV}[kind] + c * P


SQ = {"qk": 8, "dn": 15, "o": 23}
MS = {"qk": 1, "dn": 8, "o": 16}
LN = {"qk": 0, "dn": 7, "o": 15}


def chained(eng, done):
    n = [0]

    def link(ins):
        n[0] += 1
        ins.then_inc(done, 1)
        eng.wait_ge(done, n[0])
    return link


KV_OUT = 16 * (1 + 2 * (NTILE - 1) + 1 + DEC_BATCH)
LO_OUT = 16 * 6

LAYER_SEMS = """
par_in lrow_in w_in0 w_in1 w_in2 ow_in0 ow_in1 ow_in2 ow_in3 ow_in4 ow_in5 par_t sq_ok ms_ok rstd_ok h_ok pj
pa pv lam_ok lh_t u_ok lgp lg at_ok lt_ok lq_ok lru_ok lc_ok lo_t lo_ok gt_t gt_ok gs_ok nq_y nq_sw
nq_r qk_ok kt_t kt_e vc_mm c_ok c_s c_m c_e c_t c_c c_pv c_o o_sum a_s a_m a_p a_t a_ca a_cd a_v a_o
o_t z_o gq_t qb_ok ch_in0 ch_in1 s_pl s_pe s_kt s_ke s_t1 s_t2 s_t3 s_e1 s_e2 s_e3 s_sc s_pv s_cm s_ce s_cn
s_im s_wc s_m s_mw s_wm s_sm s_p s_pw s_tr s_tb s_ta s_mix s_or s_ot s_z dr_in dh_t dh_c conv_ok silu_ok dc_ok
sp_abs sp_exp gb_ok n_ok s0_in p_g p_e p_x p_d p_k p_b i_w i_wm i_x i_xm f_mm f_u f_w q_w q_v q_s q_n q_oe
b_ws b_vt b_tr b_vn b_o b_vm b_sm b_sn dn_ok po mp mg_ok v_chain a_chain done small_in ln_ok
""".split()


def hybrid_trunk(nc, dram, out):
    ctx = ExitStack()
    with ctx:
        def sb(name, shape, dt=F32):
            return ctx.enter_context(nc.sbuf_tensor(name, shape, dt))

        con = sb("con", [P, NCON])
        xT = sb("xT", [P, KT_M, T])
        hT = sb("hT", [P, KT_M, T])
        zs = sb("zs", [P, 12, T])
        ring = sb("ring", [P, RING, KT_M, GW])
        arena = sb("arena", [P, NARENA])
        par = sb("par", [P, NPAR])
        dnp = sb("dnp", [P, 2 * DN_H])
        wab = sb("wab", [P, 2, 4, P])
        gtok = sb("gtok", [P, NTILE, NSM])
        cst = sb("cst", [P, 16, 27])
        lst = sb("lst", [P, 4, 9])
        h0 = sb("h0", [P, 4, DEC_BATCH])
        sm8 = sb("sm8", [P, 12, 8])
        spb = sb("spb", [P, 6, 20])
        g4 = sb("g4", [P, NTILE, DN_H])
        lamn = sb("lamn", [P, 2, 4])
        kcp = sb("kcp", [P, KV, NCB])
        pgt = sb("pgt", [1, DEC_BATCH * PAGES], I32)
        PS = ctx.enter_context(nc.psum_tensor("PS", [P, 8, 512], F32))

        s = {n: ctx.enter_context(nc.semaphore(n)) for n in LAYER_SEMS
                               + ["con_in", "pg_in", "x_in", "x_t", "x_e", "zero", "go", "y_t", "y_e", "y_out", "kv_out", "lo_out", "S_out", "b_out"]}

        def C(name, n=None, rows=P, k=0):
            at, size = CON[name]
            n = size if n is None else n
            return con[0:rows, at + k * n:at + (k + 1) * n]

        def prm(name, k=0):
            at = PAR[name][0] + k
            return par[:, at:at + 1]

        def area(where, name, off=0):
            at, size = where[name]
            return arena[:, off + at:off + at + size]

        def zarea(name):
            at, size = A_Z[name]
            return zs[:, 8:12, :].rearrange("p c t -> p (c t)")[:, at:at + size]

        ident = C("ident")

        wsm = area(A_NSA, "ktok")[:, 0:KT_M * NSM].rearrange("p (j n) -> p j n", j=KT_M)
        prow = area(A_NSA, "ktok")[0:NPAR, 512:512 + P]
        sq8 = arena[:, 0:8 * T].rearrange("p (c t) -> p c t", c=8)
        rstd = arena[:, 8 * T:9 * T]
        lext = area(A_LRU, "ext").rearrange("p (c t) -> p c t", c=4)
        lu, la, lb, lt, lh = (area(A_LRU, n).rearrange("p (c t) -> p c t", c=4) for n in ("u", "a", "b", "t", "h"))
        lrow = area(A_LRU, "t")[0:32, 0:D_RNN]
        rowl = area(A_LRU, "ext")[0:27, 0:D_RNN].rearrange("p (c n) -> p c n", c=4)
        rowh = area(A_LRU, "ext")[0:9, D_RNN:2 * D_RNN].rearrange("p (c n) -> p c n", c=4)
        qk7 = arena[:, 0:7 * T].rearrange("p (c t) -> p c t", c=7)
        vT = area(A_NSA, "v")[:, 0:3 * T].rearrange("p (c t) -> p c t", c=3)
        pT = area(A_NSA, "v")
        ktok = area(A_NSA, "ktok").rearrange("p (t c) -> p t c", t=NTILE)
        qb = area(A_NSA, "qb").rearrange("p (b n) -> p b n", b=DEC_BATCH)
        ss = area(A_NSA, "s")[:, 0:1088]
        sw = area(A_NSA, "s")[:, 1088:1664]
        KT = area(A_NSA, "kt")
        KW = area(A_NSA, "kw")
        rs7 = area(A_NSA, "cache")[:, 0:7 * T].rearrange("p (c t) -> p c t", c=7)
        cache = area(A_NSA, "cache").rearrange("p (s g c) -> p s g c", s=2, g=PAGES)
        win = area(A_NSA, "win").rearrange("p (s g c) -> p s g c", s=2, g=4)
        pring = [area(A_NSA, "s")[:, k * 512:(k + 1) * 512] for k in range(3)]
        pTring = [area(A_NSA, "kt")[:, k * 512:(k + 1) * 512] for k in range(2)]
        otok = area(A_NSA, "kw")
        pc, pcT, otmp = pT[:, 0:P], pT[:, P:2 * P], pT[:, 2 * P:6 * P]
        gT, vcb, ckv, cpT, orow, cp, kcT, exn, eqb, gsel = (zarea(n) for n in (
            "gT", "vcb", "ckv", "cpT", "orow", "cp", "kcT", "ex", "eq", "gsel"))
        dext = area(A_DN, "ext").rearrange("p (c t) -> p c t", c=12)
        dc = area(A_DN, "c").rearrange("p (c t) -> p c t", c=12)
        dsq = arena[:, 0:8 * T].rearrange("p (c t) -> p c t", c=8)
        grp = {n: area(A_DN, n).rearrange("p (t h n) -> p t h n", t=2, h=DN_H) for n in ("qk", "kd", "u", "w")}
        tmp = {n: area(A_TMP, n).rearrange("p (t h n) -> p t h n", t=2, h=DN_H) for n in A_TMP}
        Sp = area(A_DN, "S").rearrange("p (h e) -> p h e", h=DN_H)
        S0 = area(A_DN, "S0").rearrange("p (b h e) -> p b h e", b=DEC_BATCH, h=DN_H)
        drow = area(A_DN, "S0")[0:24, 0:1536]
        rowd = area(A_DN, "S0")[0:27, 2048:2048 + 1536]
        bvm = [arena[:, k * 1024:(k + 1) * 1024] for k in range(2)]
        mT = area(A_MG, "m").rearrange("p (c t) -> p c t", c=8)
        ow = area(A_MG, "ow").rearrange("p (s k n) -> p s k n", s=6, k=4)
        sg = area(A_MG, "sg").rearrange("p (s t) -> p s t", s=2)
        mpr = area(A_MG, "pr")

        def halves(ap):
            return ap.rearrange("p (a t) -> p a t", a=2)

        def pair(b):
            return PS[:, b:b + 2, 0:HALF]

        def bank4(b, n=P, rows=P):
            return PS[0:rows, b, 0:4 * P].rearrange("p (h n) -> p h n", h=4)[:, :, 0:n]

        def bc(ap, n):
            return ap.unsqueeze(2).to_broadcast([ap.shape[0], ap.shape[1], n])

        def rep(ap, n):
            return ap.unsqueeze(1).to_broadcast([ap.shape[0], n, ap.shape[1]])

        def at_layer(name, l):
            return dram[name][bass.ds(l, 1)]

        ring_in = [s["w_in0"], s["w_in1"], s["w_in2"]]
        parts = [4 if PROJ[WIDE[2 * g]][0] in ("q", "nz") else 1 for g in range(len(WIDE) // 2)]

        def landed(g):
            return 16 * sum(n for j, n in enumerate(parts[:g + 1]) if j % RING == g % RING)

        ow_in = [s["ow_in0"], s["ow_in1"], s["ow_in2"], s["ow_in3"], s["ow_in4"], s["ow_in5"]]

        block = ctx.enter_context(nc.Block())

        @block.sync
        def _(sp):
            sp.dma_start(con[:], dram["con"]).then_inc(s["con_in"], 16)
            for k, (t, n) in enumerate(TILES):
                src = dram["x_prompt"][0, t:t + n, :] if t < SEQ else dram["x_sample"].rearrange("b t c -> (b t) c")
                sp.dma_start(arena[0:n, k * D_MODEL:(k + 1) * D_MODEL], src).then_inc(s["x_in"], 16)
            sp.dma_start(pgt[:], dram["page_table"].rearrange("b n -> (b n)").unsqueeze(0)).then_inc(s["pg_in"], 16)
            sp.wait_ge(s["pg_in"], 16)
            sp.wait_ge(s["zero"], 2)
            sp.wait_ge(s["x_e"], 10)
            with sp.Fori(0, DEPTH) as l:
                def rows(name, k, src):
                    at, n = PAR[name]
                    sp.dma_start(prow[at + k:at + k + src.shape[0], 0:src.shape[1]], src).then_inc(s["par_in"], 16)

                def vec(name, n):
                    return at_layer(name, l).rearrange("a (j p) -> (a j) p", p=n)

                def mat(name):
                    return at_layer(name, l).rearrange("a w (c p) -> (a w c) p", p=P)

                rows("gain", 0, vec("norm_gain", P))
                rows("lconv", 0, mat("lru_conv_w"))
                rows("lcb", 0, vec("lru_conv_b", P))
                rows("ba", 0, vec("lru_ba", P))
                rows("bx", 0, vec("lru_bx", P))
                rows("lam", 0, vec("lru_lambda", P))
                rows("dconv", 0, mat("dn_conv_w"))
                rows("on", 0, vec("dn_o_norm", P))
                for half in range(2):
                    at = PAR["qn"][0]
                    sp.dma_start(prow[at:at + 1, half * HD:(half + 1) * HD], vec("nsa_q_norm", HD))\
                        .then_inc(s["par_in"], 16)
                    at = PAR["kn"][0]
                    sp.dma_start(prow[at:at + 3, half * HD:(half + 1) * HD],
                                 at_layer("nsa_k_norm", l).rearrange("a b d -> (a b) d")).then_inc(s["par_in"], 16)
                for k, name in enumerate(("dn_A_log", "dn_dt_bias")):
                    sp.dma_start(dnp[:, k * DN_H:(k + 1) * DN_H], at_layer(name, l).to_broadcast([P, DN_H]))\
                        .then_inc(s["small_in"], 16)
                for k, name in enumerate(("lru_wa", "lru_wx")):
                    for odd in range(2):
                        src = at_layer(name, l).rearrange("a (c o) i d -> (a o) i c d", o=2)[odd]
                        sp.dma_start(wab[odd * HD:(odd + 1) * HD, k, :, odd * HD:(odd + 1) * HD], src)\
                            .then_inc(s["small_in"], 16)
                sp.dma_start(lrow[0:24, :], at_layer("state_lru_conv", l).rearrange("a b k c -> (a b k) c"))\
                    .then_inc(s["lrow_in"], 16)
                sp.dma_start(lrow[24:32, :], at_layer("state_lru_h", l).rearrange("a b c -> (a b) c"))\
                    .then_inc(s["lrow_in"], 16)
                w_in = at_layer("w_in", l).rearrange("a (j p) c -> p (a j) c", p=P)
                sp.dma_start(wsm[:, :, 0:NG], w_in[:, :, C_NG:C_NG + NG]).then_inc(s["small_in"], 16)
                sp.dma_start(wsm[:, :, NG:NSM], w_in[:, :, C_DA:C_DA + 2 * DN_H]).then_inc(s["small_in"], 16)

                n_ow = 0
                for g in range(len(WIDE) // 2):
                    i = WIDE[2 * g]
                    kind, c, _ = PROJ[i]
                    slot = ring[:, g % RING]
                    if (kind, c) == ("dc", 2 * RING):
                        pages = dram["cache_nsa_kv"].rearrange("l n p k g d -> (l n) p (k g d)")
                        for b in range(DEC_BATCH):
                            ch_in = (s["ch_in0"], s["ch_in1"])[b % 2]
                            if b == 0:
                                sp.wait_ge(s["qk_ok"], 7)
                            if b >= 2:
                                sp.wait_ge(s["s_pv"], b - 1)
                            for k in range(PAGES):
                                page = sp.value_load(pgt[0:1, b * PAGES + k:b * PAGES + k + 1], min_val=0, max_val=N_PHYS - 1)
                                src = pages[bass.ds(sp.snap(page + l * N_PHYS), 1)]
                                sp.dma_start(cache[:, b % 2, k, :], src.rearrange("a p c -> (a p) c")).then_inc(ch_in, 16)
                            src = at_layer("state_nsa_win", l).rearrange("a b (k p) w g d -> (a b) p k (w g d)", p=P)
                            sp.dma_start(win[:, b % 2], src[b]).then_inc(ch_in, 16)
                        sp.wait_ge(s["s_z"], 8)
                        sp.dma_start(drow, at_layer("state_dn_conv", l).rearrange("a b k c -> (a b k) c"))\
                            .then_inc(s["dr_in"], 16)
                    if (kind, c) == ("mg", 0):
                        sp.wait_ge(s["dh_c"], 1)
                        sp.wait_ge(s["lo_out"], l * LO_OUT + LO_OUT)
                        for b in range(DEC_BATCH):
                            sp.dma_start(S0[:, b], at_layer("state_dn_S", l).rearrange("a b h d e -> (a b) d h e")[b])\
                                .then_inc(s["s0_in"], 16)
                    if g >= RING:
                        sp.wait_ge(s["pj"], WIDE[2 * (g - RING) + 1] + 1)
                    if kind in ("q", "nz"):
                        base = C_Q if kind == "q" else C_NZ
                        for t in range(GT):
                            for kvh in range(KV):
                                col = base + kvh * REP * HD + (c + t) * HD
                                sp.dma_start(slot[:, :, t * P + kvh * HD:t * P + (kvh + 1) * HD],
                                             w_in[:, :, col:col + HD]).then_inc(ring_in[g % RING], 16)
                    elif kind == "wo":
                        w_out = at_layer("w_out", l).rearrange("a (j p) c -> p (a j) c", p=P)
                        sp.dma_start(slot, w_out[:, :, c * P:c * P + GW]).then_inc(ring_in[g % RING], 16)
                    else:
                        col = first_col(kind, c) if kind != "mg" else C_MG + c % 6 // 2 * D_MODEL + c // 6 * GW
                        sp.dma_start(slot, w_in[:, :, col:col + GW]).then_inc(ring_in[g % RING], 16)
                    if kind == "mg":
                        br, jj = c % 6 // 2, c // 6
                        if n_ow == 0:
                            sp.wait_ge(s["dn_ok"], 1)
                        if n_ow >= 6:
                            sp.wait_ge(s["po"], 2 * (n_ow - 6) + 2)
                        o = n_ow % 6
                        name = ("w_lru_out", "w_nsa_out", "w_dn_out")[br]
                        if br == 1:
                            for kvh in range(KV):
                                src = at_layer(name, l).rearrange("a (g r d) n -> (a g) d r n", g=KV, r=REP)[kvh]
                                sp.dma_start(ow[kvh * HD:(kvh + 1) * HD, o], src[:, :, jj * GW:(jj + 1) * GW])\
                                    .then_inc(ow_in[o], 16)
                        else:
                            src = at_layer(name, l).rearrange("a (k p) n -> p (a k) n", p=P)
                            sp.dma_start(ow[:, o], src[:, :, jj * GW:(jj + 1) * GW]).then_inc(ow_in[o], 16)
                        n_ow += 1
                sp.wait_ge(s["done"], 4)
                for name in LAYER_SEMS:
                    sp.sem_clear(s[name])
                sp.sem_inc(s["go"], 1)

        @block.gpsimd
        def _(pool):
            pool.memset(wab[:], 0.0).then_inc(s["zero"], 1)
            pool.memset(gtok[:], 0.0).then_inc(s["zero"], 1)
            with pool.Fori(0, DEPTH) as l:
                def out_l(name):
                    return out[name][bass.ds(l, 1)]

                pool.dma_start(out_l("win_sample")[:, :, 0:WINDOW - DEC_SEQ].rearrange("a b w k g d -> (a b) (w k g d)"),
                               at_layer("state_nsa_win", l)[:, :, DEC_SEQ:].rearrange("a b w k g d -> (a b) (w k g d)"))\
                    .then_inc(s["kv_out"], 16)
                pool.wait_ge(s["lo_ok"], 2)
                for name, r0, n in (("lru_conv_prompt", 0, 3), ("lru_conv_sample", 3, 24)):
                    pool.dma_start(out_l(name).rearrange("a b k c -> (a b k) c"),
                                   rowl[r0:r0 + n].rearrange("p c n -> p (c n)")).then_inc(s["lo_out"], 16)
                for name, r0, n in (("lru_h_prompt", 0, 1), ("lru_h_sample", 1, 8)):
                    pool.dma_start(out_l(name).rearrange("a b c -> (a b) c"),
                                   rowh[r0:r0 + n].rearrange("p c n -> p (c n)")).then_inc(s["lo_out"], 16)
                for k, (t, n) in enumerate(TILES):
                    pool.wait_ge(s["kt_e"], k + 1)
                    if t < SEQ:
                        dst = out_l("kv_prompt").rearrange("a b t k g d -> (a b t) (k g d)")
                        pool.dma_start(dst[t:t + n], ktok[0:n, k, 0:4 * P]).then_inc(s["kv_out"], 16)
                        dst = out_l("win_prompt").rearrange("a b t k g d -> (a b t) (k g d)")
                        pool.dma_start(dst[t:t + n], ktok[0:n, k, 4 * P:6 * P]).then_inc(s["kv_out"], 16)
                    else:
                        dst = out_l("kv_sample").rearrange("a b t k g d -> (a b t) (k g d)")
                        pool.dma_start(dst, ktok[0:n, k, 0:4 * P]).then_inc(s["kv_out"], 16)
                        dst = out_l("win_sample").rearrange("a b w k g d -> (a b) w (k g d)")
                        for b in range(DEC_BATCH):
                            pool.dma_start(dst[b, WINDOW - DEC_SEQ:], ktok[b * DEC_SEQ:(b + 1) * DEC_SEQ, k, 4 * P:6 * P])\
                                .then_inc(s["kv_out"], 16)
                pool.wait_ge(s["lo_ok"], 3)
                for name, r0, n in (("dn_conv_prompt", 0, 3), ("dn_conv_sample", 3, 24)):
                    pool.dma_start(out_l(name).rearrange("a b k c -> (a b k) c"), rowd[r0:r0 + n]).then_inc(s["lo_out"], 16)
                pool.wait_ge(s["q_n"], SEQ // CHUNK)
                pool.dma_start(out_l("dn_S_prompt").rearrange("a b h d e -> d (a b h) e"), Sp).then_inc(s["S_out"], 16)
                pool.wait_ge(s["b_sn"], DN_H)
                pool.dma_start(out_l("dn_S_sample").rearrange("a b h d e -> d (a b h) e"),
                               S0.rearrange("p b h e -> p (b h) e")).then_inc(s["b_out"], 16)
                pool.wait_ge(s["kv_out"], l * KV_OUT + KV_OUT)
                pool.wait_ge(s["lo_out"], l * LO_OUT + LO_OUT)
                pool.wait_ge(s["S_out"], l * 16 + 16)
                pool.wait_ge(s["b_out"], l * 16 + 16)
                pool.sem_inc(s["done"], 1)
                pool.wait_ge(s["go"], l + 1)
            for k, (t, n) in enumerate(TILES):
                dst = out["y_prompt"][0, t:t + n, :] if t < SEQ else out["y_sample"].rearrange("b t c -> (b t) c")
                pool.wait_ge(s["y_e"], 2 * k + 2)
                pool.dma_start(dst, arena[0:n, k * D_MODEL:(k + 1) * D_MODEL]).then_inc(s["y_out"], 16)
            pool.wait_ge(s["y_out"], 16 * NTILE)

        @block.tensor
        def _(pe):
            mm = nc.tensor.matmul

            def turn(dst, src):
                return nc.tensor.transpose(dst, src, ident[0:src.shape[0], 0:src.shape[0]])

            pe.wait_ge(s["con_in"], 16)
            pe.wait_ge(s["x_in"], 16 * NTILE)
            for k, (t, n) in enumerate(TILES):
                for h in range(2):
                    u = 2 * k + h
                    if u >= 4:
                        pe.wait_ge(s["x_e"], u - 3)
                    for c in range(4):
                        j = 4 * h + c
                        ins = turn(PS[:, u % 4, c * P:c * P + n], arena[0:n, k * D_MODEL + j * P:k * D_MODEL + (j + 1) * P])
                    ins.then_inc(s["x_t"], 1)
            pe.wait_ge(s["x_e"], 10)

            with pe.Fori(0, DEPTH) as l:
                def proj(i, src=hT):
                    kind, c, _ = PROJ[i]
                    if i >= 2:
                        who = PROJ[i - 2][2]
                        pe.wait_ge(s["pa"] if who == "A" else s["pv"], taken(i - 1, who))
                    if kind == "sm":
                        pe.wait_ge(s["small_in"], 8 * 16)
                    elif WIDE.index(i) % GT == 0:
                        g = WIDE.index(i) // GT
                        pe.wait_ge(ring_in[g % RING], landed(g))
                    for j in range(KT_M):
                        for h in range(2):
                            if kind == "sm":
                                w, dst = wsm[:, j, :], PS[0:NSM, 2 * (i % 2) + h, 0:HALF]
                            else:
                                wi = WIDE.index(i)
                                t = wi % GT
                                w = ring[:, wi // GT % RING, j, t * P:(t + 1) * P]
                                dst = PS[:, 2 * (i % 2) + h, 0:HALF]
                            ins = mm(dst, w, src[:, j, h * HALF:(h + 1) * HALF], start=j == 0, stop=j == KT_M - 1)
                    ins.then_inc(s["pj"], 1)

                pe.wait_ge(s["par_in"], 12 * 16)
                turn(PS[:, 5, 0:NPAR], prow[:]).then_inc(s["par_t"], 1)
                for j in range(KT_M):
                    pe.wait_ge(s["sq_ok"], j + 1)
                    for h in range(2):
                        ins = mm(PS[:, 6 + h, 0:HALF], C("ones"), sq8[:, j, h * HALF:(h + 1) * HALF],
                                 start=j == 0, stop=j == KT_M - 1)
                ins.then_inc(s["ms_ok"], 1)
                pe.wait_ge(s["h_ok"], KT_M)
                pe.wait_ge(s["lrow_in"], 32)
                for c in range(4):
                    ins = turn(PS[:, 6, c * 32:(c + 1) * 32], lrow[:, c * P:(c + 1) * P])
                ins.then_inc(s["lh_t"], 1)
                for i in range(LRU_AT):
                    proj(i)
                pe.wait_ge(s["small_in"], 8 * 16)
                for n in range(8):
                    c, k = n // 2, n % 2
                    pe.wait_ge(s["u_ok"], c + 1)
                    if n >= 2:
                        pe.wait_ge(s["lg"], n - 1)
                    for h in range(2):
                        ins = mm(PS[:, 4 + 2 * k + h, 0:HALF], wab[:, k, c, :], lu[:, c, h * HALF:(h + 1) * HALF],
                                 start=True, stop=True)
                    ins.then_inc(s["lgp"], 1)
                for i in range(LRU_AT, NP_NSA):
                    proj(i)
                pe.wait_ge(s["lg"], 8)
                pe.wait_ge(s["pv"], taken(NP_NSA, "V"))
                for k, (t, n) in enumerate(TILES):
                    ins = turn(PS[0:n, 4, k * NSM:(k + 1) * NSM], gT[0:NSM, t:t + n])
                ins.then_inc(s["gt_t"], 1)
                pe.wait_ge(s["lc_ok"], 1)
                for c in range(4):
                    turn(PS[0:27, 6, c * P:(c + 1) * P], cst[:, c, :])
                    ins = turn(PS[0:9, 7, c * P:(c + 1) * P], lst[:, c, :])
                ins.then_inc(s["lo_t"], 1)
                pe.wait_ge(s["gt_ok"], 2)
                pe.wait_ge(s["lo_ok"], 2)
                for n in range(7):
                    pe.wait_ge(s["sq_ok"], SQ["qk"] + n + 1)
                    if n >= 2:
                        pe.wait_ge(s["ln_ok"], LN["qk"] + n - 1)
                    for h in range(2):
                        ins = mm(PS[:, 4 + 2 * (n % 2) + h, 0:HALF], C("blk"), rs7[:, n, h * HALF:(h + 1) * HALF],
                                 start=True, stop=True)
                    ins.then_inc(s["ms_ok"], 1)
                pe.wait_ge(s["ln_ok"], LN["qk"] + 7)
                for n in range(7):
                    pe.wait_ge(s["nq_y"], n + 1)
                    if n >= 2:
                        pe.wait_ge(s["nq_r"], n - 1)
                    for h in range(2):
                        ins = mm(PS[:, 4 + 2 * (n % 2) + h, 0:HALF], C("swap"), qk7[:, n, h * HALF:(h + 1) * HALF],
                                 start=True, stop=True)
                    ins.then_inc(s["nq_sw"], 1)
                pe.wait_ge(s["nq_r"], 7)
                pe.wait_ge(s["qk_ok"], 7)
                pe.wait_ge(s["pa"], taken(NP_NSA, "A"))
                for k, (t, n) in enumerate(TILES):
                    if k >= 2:
                        pe.wait_ge(s["kt_e"], k - 1)
                    b = 4 + 2 * (k % 2)
                    flat = PS[:, b:b + 2, :].rearrange("p b n -> p (b n)")
                    for c in range(6):
                        src = (qk7[:, 4 + c // 2] if c % 2 == 0 else vT[:, c // 2])[:, t:t + n]
                        ins = turn(flat[0:n, c * P:(c + 1) * P], src)
                    ins.then_inc(s["kt_t"], 1)
                pe.wait_ge(s["kt_e"], NTILE)
                for k in range(4):
                    ins = mm(PS[:, 7, 0:P], C("poolp", P, k=k), ktok[:, k, P:2 * P], start=k == 0, stop=k == 3)
                ins.then_inc(s["vc_mm"], 1)
                pe.wait_ge(s["c_ok"], 1)

                for qt in range(4):
                    q0 = qt * P
                    if qt >= 1:
                        pe.wait_ge(s["z_o"], qt)
                    for r in range(REP):
                        ins = mm(PS[:, 7, r * KV * NCB:(r + 1) * KV * NCB], qk7[:, r, q0:q0 + P],
                                 kcp.rearrange("p g n -> p (g n)"), start=True, stop=True)
                    ins.then_inc(s["c_s"], 1)

                    def scores(u):
                        br, h = (u // HEADS) % 2, u % HEADS
                        r, g = h // KV, h % KV
                        if u >= 2:
                            pe.wait_ge(s["a_p"], u - 1)
                        mm(PS[:, 4 + u % 2, 0:q0 + P], qk7[g * HD:(g + 1) * HD, r, q0:q0 + P],
                           qk7[g * HD:(g + 1) * HD, 5 + br, 0:q0 + P], start=True, stop=True).then_inc(s["a_s"], 1)

                    def turn_p(u):
                        pe.wait_ge(s["a_p"], u + 1)
                        if u >= 2:
                            pe.wait_ge(s["a_ca"] if u % 2 == 0 else s["a_cd"], u // 2)
                        for k in range(qt + 1):
                            ins = turn(PS[:, 2 + u % 2, k * P:(k + 1) * P], pring[u % 3][:, k * P:(k + 1) * P])
                        ins.then_inc(s["a_t"], 1)

                    def values(u):
                        br, h = (u // HEADS) % 2, u % HEADS
                        g = h % KV
                        pe.wait_ge(s["a_ca"] if u % 2 == 0 else s["a_cd"], u // 2 + 1)
                        if h == 0 and u >= 2 * HEADS:
                            pe.wait_ge(s["a_o"], u // HEADS - 1)
                        col = (3 + 2 * br) * P + g * HD
                        for k in range(qt + 1):
                            ins = mm(PS[:, br, h * HD:(h + 1) * HD], pTring[u % 2][:, k * P:(k + 1) * P],
                                     ktok[:, k, col:col + HD], start=k == 0, stop=k == qt)
                        ins.then_inc(s["a_v"], 1)

                    u0 = 2 * HEADS * qt
                    for i in range(2 * HEADS + 3):
                        if i < 2 * HEADS:
                            scores(u0 + i)
                        if 2 <= i < 2 * HEADS + 2:
                            turn_p(u0 + i - 2)
                        if i >= 3:
                            values(u0 + i - 3)
                        if i == 3:
                            pe.wait_ge(s["c_e"], qt + 1)
                            turn(PS[:, 7, P:2 * P], pc).then_inc(s["c_t"], 1)
                        if i == 6:
                            pe.wait_ge(s["c_c"], qt + 1)
                            mm(PS[:, 6, 0:HEADS * HD], pcT, vcb, start=True, stop=True).then_inc(s["c_pv"], 1)
                    pe.wait_ge(s["o_sum"], qt + 1)
                    for r in range(REP):
                        ins = turn(PS[:, 6, r * P:(r + 1) * P], otok[:, r * P:(r + 1) * P])
                    ins.then_inc(s["o_t"], 1)

                pe.wait_ge(s["z_o"], 4)
                pe.wait_ge(s["gs_ok"], 2)
                for k in range(4):
                    ins = mm(PS[:, 5, 256 + k * NG:256 + (k + 1) * NG], C("sel", P, rows=T_S, k=k),
                             gtok[0:T_S, 4, 0:NG], start=True, stop=True)
                ins.then_inc(s["gq_t"], 1)
                pe.wait_ge(s["qb_ok"], 3)
                for b in range(DEC_BATCH):
                    k2, b2 = b // 2, b % 2
                    rows_ = slice(64 * b2, 64 * b2 + 64)
                    pe.wait_ge((s["ch_in0"], s["ch_in1"])[b2], 16 * (PAGES + 1) * (k2 + 1))
                    if b2 == 0 and k2 >= 1:
                        pe.wait_ge(s["s_z"], 2 * k2)
                    for k in range(PAGES):
                        at = CON["poolz"][0] + 4 * (PAGES - 1 - k)
                        ins = mm(PS[0:NPB, 7, 0:2 * P], con[:, at:at + NPB], cache[:, b2, k, 0:2 * P],
                                 start=k == 0, stop=k == PAGES - 1)
                    ins.then_inc(s["s_pl"], 1)
                    for c in range(2):
                        if b >= 1:
                            pe.wait_ge((s["s_e1"], s["s_e2"])[c], b)
                        if b2 == 0 and k2 >= 1:
                            pe.wait_ge((s["s_ta"], s["s_tb"])[c], k2)
                        for k in range(4):
                            ins = turn(PS[:, 2 + c, k * P:(k + 1) * P], cache[:, b2, 4 * c + k, 2 * P:3 * P])
                        ins.then_inc((s["s_t1"], s["s_t2"])[c], 1)
                    if b >= 1:
                        pe.wait_ge(s["s_e3"], b)
                    for k in range(4):
                        ins = turn(PS[:, 6, k * P:(k + 1) * P], win[:, b2, k, 0:P])
                    ins.then_inc(s["s_t3"], 1)
                    pe.wait_ge(s["s_pe"], b + 1)
                    turn(PS[:, 7, 256:256 + NPB], ckv[0:NPB, b2 * 2 * P:b2 * 2 * P + P]).then_inc(s["s_kt"], 1)
                    q = qb[:, b, :]
                    pe.wait_ge(s["s_e1"], b + 1)
                    mm(PS[rows_, 0, :], q, KT[:, 0:512], start=True, stop=True)
                    pe.wait_ge(s["s_e2"], b + 1)
                    mm(PS[rows_, 1, :], q, KT[:, 512:1024], start=True, stop=True)
                    pe.wait_ge(s["s_e3"], b + 1)
                    mm(PS[rows_, 4, :], q, KW, start=True, stop=True)
                    mm(PS[rows_, 5, 0:T_S], q, qk7[:, 5, SEQ:T], start=True, stop=True)
                    mm(PS[rows_, 5, T_S:2 * T_S], q, qk7[:, 6, SEQ:T], start=True, stop=True)
                    pe.wait_ge(s["s_ke"], b + 1)
                    mm(PS[rows_, 5, P:P + NPB], q, kcT, start=True, stop=True).then_inc(s["s_sc"], 1)
                    if b2 == 0:
                        continue
                    pe.wait_ge(s["s_cn"], k2 + 1)
                    mm(PS[:, 7, 288:288 + NPB], C("rsum"), cp, start=True, stop=True).then_inc(s["s_im"], 1)
                    pe.wait_ge(s["s_pw"], k2 + 1)
                    pe.wait_ge(s["s_e3"], b + 1)
                    for k in range(4):
                        ins = turn(PS[:, 6, k * P:(k + 1) * P], sw[:, k * P:(k + 1) * P])
                    ins.then_inc(s["s_wc"], 1)
                    pe.wait_ge(s["s_p"], k2 + 1)
                    for c in range(2):
                        for k in range(4):
                            ins = turn(PS[:, 2 + c, k * P:(k + 1) * P], ss[:, (4 * c + k) * P:(4 * c + k + 1) * P])
                        ins.then_inc(s["s_tr"], 1)
                    turn(PS[0:T_S, 7, 0:P], ss[:, 1024:1088])
                    turn(PS[0:T_S, 7, P:2 * P], sw[:, 512:576])
                    turn(PS[0:NPB, 7, 2 * P:3 * P], cp).then_inc(s["s_m"], 1)
                    pe.wait_ge(s["s_mix"], k2 + 1)
                    pe.wait_ge(s["s_ta"], k2 + 1)
                    pe.wait_ge(s["s_tb"], k2 + 1)
                    pe.wait_ge(s["s_mw"], k2 + 1)
                    for bb in range(2):
                        m = slice(64 * bb, 64 * bb + 64)
                        for k in range(PAGES):
                            mm(PS[m, 4, 0:P], pT[:, k * P + 64 * bb:k * P + 64 * bb + 64], cache[:, bb, k, 3 * P:4 * P],
                               start=k == 0, stop=False)
                        mm(PS[m, 4, 0:P], pT[0:T_S, 1536 + 64 * bb:1536 + 64 * bb + 64], ktok[0:T_S, 4, 3 * P:4 * P],
                           start=False, stop=True)
                        for k in range(4):
                            at = 1024 + k * P + 64 * bb
                            mm(PS[m, 4, P:2 * P], pT[:, at:at + 64], win[:, bb, k, P:2 * P], start=k == 0, stop=False)
                        mm(PS[m, 4, P:2 * P], pT[0:T_S, 1664 + 64 * bb:1664 + 64 * bb + 64],
                           ktok[0:T_S, 4, 5 * P:6 * P], start=False, stop=True)
                        mm(PS[m, 4, 2 * P:3 * P], cpT[0:NPB, 64 * bb:64 * bb + 64],
                           ckv[0:NPB, bb * 2 * P + P:bb * 2 * P + 2 * P], start=True, stop=True).then_inc(s["s_pv"], 1)
                    pe.wait_ge(s["s_or"], k2 + 1)
                    turn(PS[:, 5, 0:P], orow).then_inc(s["s_ot"], 1)

                pe.wait_ge(s["s_z"], 8)
                for i in range(NP_NSA, NP_DN):
                    if i == NP_NSA + 1:
                        pe.wait_ge(s["dr_in"], 16)
                        for c in range(12):
                            ins = turn(PS[:, 4, c * 24:(c + 1) * 24], drow[:, c * P:(c + 1) * P])
                        ins.then_inc(s["dh_t"], 1)
                    proj(i)
                pe.wait_ge(s["dc_ok"], 1)
                for c in range(12):
                    ins = turn(PS[0:27, 5 + c // 4, c % 4 * P:(c % 4 + 1) * P], cst[:, 4 + c, :])
                ins.then_inc(s["lo_t"], 1)
                pe.wait_ge(s["lo_ok"], 3)
                pe.wait_ge(s["dh_c"], 1)
                for n in range(8):
                    pe.wait_ge(s["sq_ok"], SQ["dn"] + n + 1)
                    if n >= 2:
                        pe.wait_ge(s["ln_ok"], LN["dn"] + n - 1)
                    for h in range(2):
                        ins = mm(PS[:, 4 + 2 * (n % 2) + h, 0:HALF], C("ones"), dsq[:, n, h * HALF:(h + 1) * HALF],
                                 start=True, stop=True)
                    ins.then_inc(s["ms_ok"], 1)
                pe.wait_ge(s["n_ok"], 8)
                pe.wait_ge(s["gb_ok"], 1)
                pe.wait_ge(s["pa"], taken(NP_DN, "A"))
                pe.wait_ge(s["pv"], taken(NP_DN, "V"))

                def dn_heads(dst, f):
                    for h in range(DN_H):
                        ins = f(dst, h)
                    return ins

                done_tiles = 0
                n_iw = n_ix = n_fu = 0
                for group in DN_GROUPS:
                    for li, k in enumerate(group):
                        t, n = TILES[k]
                        sfx = "" if t < SEQ else "s"
                        U, R, I = (C(x, P)[0:n, 0:n] for x in ("U" + sfx, "R" + sfx, "ident"))
                        qs, ks, vs = (lambda h: dc[:, h, t:t + n]), (lambda h: dc[:, 4 + h, t:t + n]), \
                            (lambda h: dc[:, 8 + h, t:t + n])
                        if done_tiles:
                            pe.wait_ge(s["p_b"], done_tiles)
                            pe.wait_ge(s["p_k"], 3 * done_tiles)
                        if li == 0 and k > 0:
                            pe.wait_ge(s["q_n"], k * 2)
                            pe.wait_ge(s["q_oe"], k * 2)
                        mm(PS[0:n, 6, 0:DN_H], U, g4[0:n, k, :], start=True, stop=True)
                        mm(PS[0:n, 6, DN_H:2 * DN_H], R, g4[0:n, k, :], start=True, stop=True)
                        for h in range(DN_H):
                            ins = mm(PS[:, 0, h * P:h * P + n], g4[0:n, k, h:h + 1].to_broadcast([n, P]), U,
                                     start=True, stop=True)
                        ins.then_inc(s["p_g"], 1)
                        for h in range(DN_H):
                            mm(PS[0:n, 2, h * P:h * P + n], ks(h), ks(h), start=True, stop=True)
                            mm(PS[0:n, 3, h * P:h * P + n], ks(h), qs(h), start=True, stop=True)
                            ins = mm(PS[0:n, 1, h * P:h * P + n], gtok[0:n, k, NG + DN_H + h:NG + DN_H + h + 1]
                                     .to_broadcast([n, n]), I, start=True, stop=True)
                        ins.then_inc(s["p_g"], 1)
                        for h in range(DN_H):
                            turn(PS[0:n, 4, h * P:(h + 1) * P], ks(h))
                            ins = turn(PS[0:n, 5, h * P:(h + 1) * P], vs(h))
                        ins.then_inc(s["p_g"], 1)
                        done_tiles += 1
                    pe.wait_ge(s["p_b"], done_tiles)
                    pe.wait_ge(s["p_k"], 3 * done_tiles)
                    levels = 6 if TILES[group[0]][0] < SEQ else 3
                    for lev in range(levels):
                        for li, k in enumerate(group):
                            n = TILES[k][1]
                            if lev:
                                pe.wait_ge(s["i_xm"], n_ix - len(group) + li + 1)
                            for h in range(DN_H):
                                x = ident[0:n, 0:n] if lev == 0 else tmp["X"][0:n, li, h, 0:n]
                                ins = mm(PS[0:n, li, h * P:h * P + n], tmp["B"][0:n, li, h, 0:n], x, start=True, stop=True)
                            ins.then_inc(s["i_w"], 1)
                        for li, k in enumerate(group):
                            n = TILES[k][1]
                            pe.wait_ge(s["i_wm"], n_iw + li + 1)
                            for h in range(DN_H):
                                w = tmp["W"][0:n, li, h, 0:n]
                                y = ident[0:n, 0:n] if lev == 0 else tmp["Y"][0:n, li, h, 0:n]
                                if 0 < lev < levels - 1:
                                    mm(PS[0:n, 2 + li, h * P:h * P + n], y, w, start=True, stop=True)
                                ins = mm(PS[0:n, 4 + li, h * P:h * P + n], w, y, start=True, stop=True)
                            ins.then_inc(s["i_x"], 1)
                        n_iw += len(group)
                        n_ix += len(group)
                    for li, k in enumerate(group):
                        t, n = TILES[k]
                        pe.wait_ge(s["i_xm"], n_ix - len(group) + li + 1)
                        for h in range(DN_H):
                            y = tmp["Y"][0:n, li, h, 0:n]
                            if t < SEQ:
                                mm(PS[0:n, 6, h * P:(h + 1) * P], y, tmp["bv"][0:n, li, h, :], start=True, stop=True)
                            else:
                                mm(PS[:, 6, h * P:h * P + n], tmp["bv"][0:n, li, h, :], y, start=True, stop=True)
                            ins = mm(PS[:, 7, h * P:h * P + n], tmp["kb"][0:n, li, h, :], y, start=True, stop=True)
                        ins.then_inc(s["f_mm"], 1)
                        n_fu += 1
                        pe.wait_ge(s["f_u"], n_fu)
                        pe.wait_ge(s["f_w"], n_fu)
                    if TILES[group[0]][0] < SEQ:
                        for li, k in enumerate(group):
                            for half in range(2):
                                c = 2 * k + half
                                rw = slice(half * CHUNK, (half + 1) * CHUNK)
                                cols = slice(c * CHUNK, (c + 1) * CHUNK)
                                pe.wait_ge(s["q_n"], c)
                                for h in range(DN_H):
                                    ins = mm(PS[rw, 0, h * P:(h + 1) * P], grp["w"][:, li, h, rw], Sp[:, h, :],
                                             start=True, stop=True)
                                ins.then_inc(s["q_w"], 1)
                                if c:
                                    pe.wait_ge(s["q_oe"], c)
                                pe.wait_ge(s["q_v"], c + 1)
                                for h in range(DN_H):
                                    mm(PS[:, 2, h * P:(h + 1) * P], grp["kd"][rw, li, h, :], grp["u"][rw, li, h, :],
                                       start=True, stop=True)
                                    mm(PS[:, 1, h * CHUNK:(h + 1) * CHUNK], Sp[:, h, :], dc[:, h, cols],
                                       start=True, stop=False)
                                    ins = mm(PS[:, 1, h * CHUNK:(h + 1) * CHUNK], grp["u"][rw, li, h, :],
                                             grp["qk"][rw, li, h, rw], start=False, stop=True)
                                ins.then_inc(s["q_s"], 1)
                    else:
                        pe.wait_ge(s["s0_in"], 16 * DEC_BATCH)
                        for h in range(DN_H):
                            for b in range(DEC_BATCH):
                                cols = slice(b * DEC_SEQ, (b + 1) * DEC_SEQ)
                                ins = mm(PS[:, 0, h * T_S + b * DEC_SEQ:h * T_S + (b + 1) * DEC_SEQ], S0[:, b, h, :],
                                         grp["w"][:, 0, h, cols], start=True, stop=True)
                        ins.then_inc(s["b_ws"], 1)
                        pe.wait_ge(s["b_vt"], 1)
                        for h in range(DN_H):
                            ins = turn(PS[0:T_S, 2, h * P:(h + 1) * P], tmp["W"][:, 0, h, 0:T_S])
                        ins.then_inc(s["b_tr"], 1)
                        pe.wait_ge(s["b_vn"], 1)
                        for h in range(DN_H):
                            mm(PS[:, 1, h * T_S:(h + 1) * T_S], grp["u"][0:T_S, 0, h, :], grp["qk"][0:T_S, 0, h, 0:T_S],
                               start=True, stop=False, skip_group_check=True)
                            for b in range(DEC_BATCH):
                                cols = slice(SEQ + b * DEC_SEQ, SEQ + (b + 1) * DEC_SEQ)
                                ins = mm(PS[:, 1, h * T_S + b * DEC_SEQ:h * T_S + (b + 1) * DEC_SEQ], S0[:, b, h, :],
                                         dc[:, h, cols], start=False, stop=b == DEC_BATCH - 1, skip_group_check=True)
                        ins.then_inc(s["b_o"], 1)
                        for h in range(DN_H):
                            pe.wait_ge(s["b_vm"], h + 1)
                            for c in range(2):
                                ins = mm(PS[:, 4 + 2 * (h % 2) + c, :], grp["kd"][0:T_S, 0, h, :],
                                         bvm[h % 2][0:T_S, c * 512:(c + 1) * 512], start=True, stop=True)
                            ins.then_inc(s["b_sm"], 1)
                pe.wait_ge(s["b_sn"], DN_H)
                for n in range(DN_H):
                    pe.wait_ge(s["sq_ok"], SQ["o"] + n + 1)
                    if n >= 2:
                        pe.wait_ge(s["ln_ok"], LN["o"] + n - 1)
                    for h in range(2):
                        ins = mm(PS[:, 4 + 2 * (n % 2) + h, 0:HALF], C("ones"), dc[:, 4 + n, h * HALF:(h + 1) * HALF],
                                 start=True, stop=True)
                    ins.then_inc(s["ms_ok"], 1)
                pe.wait_ge(s["ln_ok"], LN["o"] + DN_H)
                pe.wait_ge(s["dn_ok"], 1)
                for c in range(24):
                    proj(NP_DN + c)
                    br, t, n_ow = c % 6 // 2, c % 2, c // 2
                    if t == 0:
                        pe.wait_ge(ow_in[n_ow % 6], sum(32 if m % 3 == 1 else 16 for m in range(n_ow + 1) if m % 6 == n_ow % 6))
                    if c >= 2:
                        pe.wait_ge(s["mp"], c - 1)
                    for k in range(4):
                        for h in range(2):
                            ins = mm(PS[:, 4 + 2 * (c % 2) + h, 0:HALF], ow[:, n_ow % 6, k, t * P:(t + 1) * P],
                                     zs[:, 4 * br + k, h * HALF:(h + 1) * HALF], start=k == 0, stop=k == 3)
                    ins.then_inc(s["po"], 1)
                pe.wait_ge(s["mg_ok"], 8)
                for i in range(NP_MG, len(PROJ)):
                    proj(i, src=mT)
                pe.sem_inc(s["done"], 1)
                pe.wait_ge(s["go"], l + 1)
            for k, (t, n) in enumerate(TILES):
                for h in range(2):
                    u = 2 * k + h
                    if u >= 4:
                        pe.wait_ge(s["y_e"], u - 3)
                    for c in range(4):
                        ins = turn(PS[0:n, u % 4, c * P:(c + 1) * P], xT[:, 4 * h + c, t:t + n])
                    ins.then_inc(s["y_t"], 1)

        def ext_parts(ext, b):
            return [(ext[:, HIST:HIST + HALF], PS[:, b, 0:HALF]),
                    (ext[:, HIST + HALF:HIST + SEQ], PS[:, b + 1, 0:SEQ - HALF]),
                    (ext[:, HIST + SEQ:EXT].rearrange("p (b t) -> p b t", t=S_EXT)[:, :, HIST:],
                     PS[:, b + 1, SEQ - HALF:HALF].rearrange("p (b t) -> p b t", t=DEC_SEQ))]

        @block.scalar
        def _(act):
            A = nc.scalar.activation
            act.wait_ge(s["x_e"], 10)
            with act.Fori(0, DEPTH) as l:
                link = chained(act, s["a_chain"])
                for j in range(KT_M):
                    A(sq8[:, j], xT[:, j], ACT.Square).then_inc(s["sq_ok"], 1)
                act.wait_ge(s["ms_ok"], 1)
                link(A(halves(rstd), pair(6), ACT.Ln, bias=C("eps"), scale=1.0 / D_MODEL))
                A(rstd, rstd, ACT.Exp, scale=-0.5).then_inc(s["rstd_ok"], 1)
                act.wait_ge(s["sp_abs"], 1)
                A(spb[:, 1, 0:4], spb[:, 0, 0:4], ACT.Exp, scale=-1.0).then_inc(s["sp_exp"], 1)

                def take(i):
                    kind, c, who = PROJ[i]
                    if who != "A":
                        return
                    act.wait_ge(s["pj"], i + 1)
                    b = 2 * (i % 2)
                    if kind in ("lz", "nz", "dz"):
                        A(halves(zs[:, {"lz": 0, "nz": 4, "dz": 8}[kind] + c]), pair(b), ACT.Silu).then_inc(s["pa"], 1)
                    elif kind == "kv":
                        A(halves(qk7[:, 4 + c // 2] if c % 2 == 0 else vT[:, c // 2]), pair(b), ACT.Copy)\
                            .then_inc(s["pa"], 1)
                    elif kind == "dc":
                        for dst, src in ext_parts(dext[:, c], b):
                            ins = A(dst, src, ACT.Copy)
                        ins.then_inc(s["pa"], 1)
                    elif kind == "mg":
                        if c >= 2:
                            act.wait_ge(s["mp"], c - 1)
                        A(halves(sg[:, c % 2]), pair(b), ACT.Sigmoid).then_inc(s["pa"], 1)

                for i in range(LRU_AT):
                    take(i)
                for n in range(8):
                    act.wait_ge(s["lgp"], n + 1)
                    A(halves((la, lb)[n % 2][:, n // 2]), pair(4 + 2 * (n % 2)), ACT.Sigmoid,
                      bias=prm(("ba", "bx")[n % 2], n // 2)).then_inc(s["lg"], 1)
                act.wait_ge(s["lam_ok"], 1)
                act.wait_ge(s["lg"], 8)
                for c in range(4):
                    A(lt[:, c], la[:, c], ACT.Tanh, scale=lamn[:, 0, c:c + 1])
                for c in range(4):
                    ins = A(la[:, c], la[:, c], ACT.Exp, scale=lamn[:, 1, c:c + 1])
                ins.then_inc(s["at_ok"], 1)
                take(LRU_AT)
                take(LRU_AT + 1)
                act.wait_ge(s["lt_ok"], 1)
                A(lt[:], lt[:], ACT.Sqrt).then_inc(s["lq_ok"], 1)
                for i in range(LRU_AT + 2, NP_NSA):
                    take(i)
                act.wait_ge(s["gt_ok"], 2)
                A(gtok[:, :, 0:NG], gtok[:, :, 0:NG], ACT.Sigmoid).then_inc(s["gs_ok"], 1)
                A(gtok[:, :, NG + DN_H:NSM], gtok[:, :, NG + DN_H:NSM], ACT.Sigmoid).then_inc(s["gs_ok"], 1)
                act.wait_ge(s["pv"], taken(NP_NSA, "V"))
                act.wait_ge(s["pa"], taken(NP_NSA, "A"))
                act.wait_ge(s["lc_ok"], 1)
                for n in range(7):
                    A(rs7[:, n], qk7[:, n], ACT.Square).then_inc(s["sq_ok"], 1)
                for n in range(7):
                    act.wait_ge(s["ms_ok"], MS["qk"] + n + 1)
                    A(halves(rs7[:, n]), pair(4 + 2 * (n % 2)), ACT.Ln, bias=C("eps"), scale=1.0 / HD)\
                        .then_inc(s["ln_ok"], 1)
                act.wait_ge(s["ln_ok"], LN["qk"] + 7)
                A(rs7[:], rs7[:], ACT.Exp, scale=-0.5).then_inc(s["rstd_ok"], 1)
                for k, (t, n) in enumerate(TILES):
                    act.wait_ge(s["kt_t"], k + 1)
                    b = 4 + 2 * (k % 2)
                    A(ktok[0:n, k, :], PS[0:n, b:b + 2, :].rearrange("p b n -> p (b n)")[:, 0:6 * P], ACT.Copy)\
                        .then_inc(s["kt_e"], 1)
                act.wait_ge(s["lo_out"], l * LO_OUT + 64)
                for qt in range(4):
                    width = (qt + 1) * P
                    act.wait_ge(s["c_m"], qt + 1)
                    A(pc, pc, ACT.Exp).then_inc(s["c_e"], 1)
                    if qt:
                        act.wait_ge(s["a_o"], 2 * qt)
                    for i in range(2 * HEADS + 2):
                        u = 2 * HEADS * qt + i
                        if i < 2 * HEADS:
                            act.wait_ge(s["a_m"], u + 1)
                            if u >= 3:
                                act.wait_ge(s["a_t"], u - 2)
                            A(pring[u % 3][:, 0:width], PS[:, 4 + u % 2, 0:width], ACT.Exp,
                              bias=sm8[:, 0, u % 4:u % 4 + 1],
                              accum_out=sm8[:, 1 + i // HEADS, i % HEADS:i % HEADS + 1]).then_inc(s["a_p"], 1)
                        v = u - 2
                        if i >= 2 and v % 2 == 0:
                            act.wait_ge(s["a_t"], v + 1)
                            if v >= 2:
                                act.wait_ge(s["a_v"], v - 1)
                            A(pTring[0][:, 0:width], PS[:, 2, 0:width], ACT.Copy).then_inc(s["a_ca"], 1)
                for b in range(DEC_BATCH):
                    k2, b2 = b // 2, b % 2
                    act.wait_ge(s["s_pl"], b + 1)
                    A(ckv[0:NPB, b2 * 2 * P:(b2 + 1) * 2 * P], PS[0:NPB, 7, 0:2 * P], ACT.Copy).then_inc(s["s_pe"], 1)
                    act.wait_ge(s["s_t1"], b + 1)
                    if b:
                        act.wait_ge(s["s_sc"], b)
                    A(KT[:, 0:512], PS[:, 2, :], ACT.Copy).then_inc(s["s_e1"], 1)
                    if b2 == 0:
                        continue
                    act.wait_ge(s["s_cm"], k2 + 1)
                    A(cp, PS[:, 5, P:P + NPB], ACT.Exp, bias=sm8[:, 5, 0:1], accum_out=sm8[:, 5, 1:2]).then_inc(s["s_ce"], 1)
                    act.wait_ge(s["s_wm"], k2 + 1)
                    A(sw, sw, ACT.Exp, bias=sm8[:, 6, 0:1], accum_out=sm8[:, 6, 1:2]).then_inc(s["s_pw"], 1)
                    act.wait_ge(s["s_sm"], k2 + 1)
                    A(ss, ss, ACT.Exp, bias=sm8[:, 7, 0:1], accum_out=sm8[:, 7, 1:2]).then_inc(s["s_p"], 1)
                    act.wait_ge(s["s_tr"], 2 * k2 + 1)
                    A(pT[:, 0:512], PS[:, 2, :], ACT.Copy).then_inc(s["s_ta"], 1)
                    act.wait_ge(s["s_m"], k2 + 1)
                    A(pT[0:T_S, 1536:1792], PS[0:T_S, 7, 0:2 * P], ACT.Copy)
                    A(cpT[0:NPB, :], PS[0:NPB, 7, 2 * P:3 * P], ACT.Copy).then_inc(s["s_mix"], 1)
                act.wait_ge(s["s_z"], 8)
                act.wait_ge(s["kv_out"], l * KV_OUT + KV_OUT)
                for c in range(12 + 2):
                    if c < 12:
                        take(NP_NSA + c)
                    if c >= 2:
                        act.wait_ge(s["conv_ok"], c - 1)
                        A(dc[:, c - 2], dc[:, c - 2], ACT.Silu).then_inc(s["silu_ok"], 1)
                for i in range(NP_NSA + 12, NP_DN):
                    take(i)
                act.wait_ge(s["sp_abs"], 2)
                A(spb[:, 1, :], spb[:, 0, :], ACT.Exp, scale=-1.0).then_inc(s["sp_exp"], 1)
                A(dnp[:, 0:DN_H], dnp[:, 0:DN_H], ACT.Exp).then_inc(s["sp_exp"], 1)
                act.wait_ge(s["dc_ok"], 1)
                act.wait_ge(s["silu_ok"], 8)
                for n in range(8):
                    A(dsq[:, n], dc[:, n], ACT.Square).then_inc(s["sq_ok"], 1)
                for n in range(8):
                    act.wait_ge(s["ms_ok"], MS["dn"] + n + 1)
                    A(halves(dsq[:, n]), pair(4 + 2 * (n % 2)), ACT.Ln, bias=C("eps")).then_inc(s["ln_ok"], 1)
                act.wait_ge(s["ln_ok"], LN["dn"] + 8)
                A(dsq[:], dsq[:], ACT.Exp, scale=-0.5).then_inc(s["rstd_ok"], 1)
                act.wait_ge(s["n_ok"], 8)
                n_f = 0
                for group in DN_GROUPS:
                    for li, k in enumerate(group):
                        t, n = TILES[k]
                        act.wait_ge(s["p_g"], 3 * k + 1)
                        A(tmp["E"][:, li, :, 0:n], bank4(0, n), ACT.Exp)
                        A(sm8[0:n, 9, :], PS[0:n, 6, 0:2 * DN_H], ACT.Exp).then_inc(s["p_e"], 1)
                        act.wait_ge(s["p_x"], k + 1)
                        A(tmp["W"][0:n, li, :, 0:n], tmp["W"][0:n, li, :, 0:n], ACT.Exp).then_inc(s["p_d"], 1)
                    for li, k in enumerate(group):
                        t, n = TILES[k]
                        n_f += 1
                        act.wait_ge(s["f_mm"], n_f)
                        A(grp["w"][:, li, :, 0:n], bank4(7, n), ACT.Copy).then_inc(s["f_w"], 1)
                    for li, k in enumerate(group):
                        t, n = TILES[k]
                        if t >= SEQ:
                            act.wait_ge(s["b_o"], 1)
                            link(A(dc[:, 0:4, t:t + n], PS[:, 1, 0:DN_H * n].rearrange("p (h n) -> p h n", h=DN_H), ACT.Copy))
                            continue
                        for c in (2 * k, 2 * k + 1):
                            act.wait_ge(s["q_s"], c + 1)
                            A(dc[:, 0:4, c * CHUNK:(c + 1) * CHUNK],
                              PS[:, 1, 0:DN_H * CHUNK].rearrange("p (h n) -> p h n", h=DN_H), ACT.Copy).then_inc(s["q_oe"], 1)
                for n in range(DN_H):
                    A(dc[:, 4 + n], dc[:, n], ACT.Square).then_inc(s["sq_ok"], 1)
                for n in range(DN_H):
                    act.wait_ge(s["ms_ok"], MS["o"] + n + 1)
                    A(halves(dc[:, 4 + n]), pair(4 + 2 * (n % 2)), ACT.Ln, bias=C("eps"), scale=1.0 / DN_D)\
                        .then_inc(s["ln_ok"], 1)
                act.wait_ge(s["ln_ok"], LN["o"] + DN_H)
                A(dc[:, 4:8], dc[:, 4:8], ACT.Exp, scale=-0.5).then_inc(s["rstd_ok"], 1)
                act.wait_ge(s["dn_ok"], 1)
                for i in range(NP_DN, NP_MG):
                    take(i)
                act.wait_ge(s["pa"], taken(len(PROJ), "A"))
                act.sem_inc(s["done"], 1)
                act.wait_ge(s["go"], l + 1)

        @block.vector
        def _(dve):
            V = nc.vector
            stt = V.scalar_tensor_tensor

            def mul(dst, a, b):
                return V.tensor_tensor(dst, a, b, ALU.mult)

            def add(dst, a, b):
                return V.tensor_tensor(dst, a, b, ALU.add)

            def sub(dst, a, b):
                return V.tensor_tensor(dst, a, b, ALU.subtract)

            dve.wait_ge(s["con_in"], 16)
            for k, (t, n) in enumerate(TILES):
                for h in range(2):
                    u = 2 * k + h
                    dve.wait_ge(s["x_t"], u + 1)
                    V.tensor_copy(xT[:, 4 * h:4 * h + 4, t:t + n], bank4(u % 4, n)).then_inc(s["x_e"], 1)
            dve.wait_ge(s["x_e"], 10)

            with dve.Fori(0, DEPTH) as l:
                link = chained(dve, s["v_chain"])

                def softplus_tail(n):
                    x, y, d, z, q = (spb[:, i, 0:n] for i in (5, 1, 2, 3, 4))
                    link(V.tensor_scalar(d, y, 2.0, None, ALU.add))
                    link(V.reciprocal(d, d))
                    link(mul(z, y, d))
                    link(mul(d, z, z))
                    link(V.tensor_scalar(q, d, 1.0 / 17, None, ALU.mult))
                    for k in (15, 13, 11, 9, 7, 5, 3):
                        link(stt(out=q, in0=q, scalar=1.0 / k, in1=d, op0=ALU.add, op1=ALU.mult))
                    link(stt(out=q, in0=q, scalar=1.0, in1=z, op0=ALU.add, op1=ALU.mult))
                    link(V.tensor_scalar(x, x, 0.0, None, ALU.max))
                    link(stt(out=q, in0=q, scalar=2.0, in1=x, op0=ALU.mult, op1=ALU.add))

                def conv(dst, ext, w, bias, done):
                    es = ext[:, HIST + SEQ:EXT].rearrange("p (b t) -> p b t", t=S_EXT)
                    ds = dst[:, SEQ:T].rearrange("p (b t) -> p b t", t=DEC_SEQ)
                    for j in range(CONV_W):
                        for k, (d, e) in enumerate(((dst[:, 0:SEQ], ext[:, j:j + SEQ]), (ds, es[:, :, j:j + DEC_SEQ]))):
                            if j:
                                ins = stt(out=d, in0=e, scalar=w(j), in1=d, op0=ALU.mult, op1=ALU.add)
                            elif bias is not None:
                                ins = V.tensor_scalar(d, e, w(j), bias, ALU.mult, ALU.add)
                            else:
                                ins = V.tensor_scalar(d, e, w(j), None, ALU.mult)
                            if j == CONV_W - 1 and k == 1:
                                ins.then_inc(done, 1)
                            else:
                                link(ins)

                dve.wait_ge(s["par_t"], 1)
                link(V.tensor_copy(par[:], PS[:, 5, 0:NPAR]))
                lam = par[:, PAR["lam"][0]:PAR["lam"][0] + 4]
                link(V.tensor_scalar(spb[:, 5, 0:4], lam, -1.0, None, ALU.mult))
                stt(out=spb[:, 0, 0:4], in0=lam, scalar=-1.0, in1=lam, op0=ALU.mult, op1=ALU.max).then_inc(s["sp_abs"], 1)
                V.tensor_scalar(prm("qn"), prm("qn"), HD ** -0.5, None, ALU.mult)
                dve.wait_ge(s["rstd_ok"], 1)
                for j in range(KT_M):
                    stt(out=hT[:, j], in0=xT[:, j], scalar=prm("gain", j), in1=rstd, op0=ALU.mult, op1=ALU.mult)\
                        .then_inc(s["h_ok"], 1)
                dve.wait_ge(s["sp_exp"], 1)
                softplus_tail(4)
                link(V.tensor_scalar(lamn[:, 0, :], spb[:, 4, 0:4], 8.0, None, ALU.mult))
                V.tensor_scalar(lamn[:, 1, :], spb[:, 4, 0:4], -8.0, None, ALU.mult).then_inc(s["lam_ok"], 1)
                V.memset(lext[:, :, 0:HIST], 0.0)
                dve.wait_ge(s["lh_t"], 1)
                rows = PS[:, 6, 0:P].rearrange("p (c n) -> p c n", c=4)
                for c in range(4):
                    V.tensor_copy(lext[:, c, HIST + SEQ:EXT].rearrange("p (b t) -> p b t", t=S_EXT)[:, :, 0:HIST],
                                  rows[:, c, 0:24].rearrange("p (b t) -> p b t", t=HIST))
                V.tensor_copy(h0[:], rows[:, :, 24:32])

                def take(i):
                    kind, c, who = PROJ[i]
                    if who != "V":
                        return
                    dve.wait_ge(s["pj"], i + 1)
                    b = 2 * (i % 2)
                    if kind in ("lx", "dc"):
                        for dst, src in ext_parts((lext if kind == "lx" else dext)[:, c], b):
                            ins = V.tensor_copy(dst, src)
                    elif kind == "q":
                        ins = V.tensor_copy(halves(qk7[:, c]), pair(b))
                    elif kind == "sm":
                        ins = V.tensor_copy(halves(gT[0:NSM, :]), PS[0:NSM, b:b + 2, 0:HALF])
                    else:
                        ins = add(halves(xT[:, c]), halves(xT[:, c]), pair(b))
                    ins.then_inc(s["pv"], 1)

                for i in range(4):
                    take(i)
                dve.wait_ge(s["pv"], 4)
                for c in range(4):
                    conv(lu[:, c], lext[:, c], lambda j: prm("lconv", 4 * j + c), prm("lcb", c), s["u_ok"])
                for i in range(4, 12):
                    take(i)
                def tails(dst, ext, n):
                    V.tensor_copy(dst[:, :, 0:HIST], ext[:, :, SEQ:SEQ + HIST])
                    for c in range(n):
                        ins = V.tensor_copy(dst[:, c, HIST:27].rearrange("p (b t) -> p b t", t=HIST),
                                            ext[:, c, HIST + SEQ:EXT].rearrange("p (b t) -> p b t", t=S_EXT)[:, :, DEC_SEQ:])
                    return ins

                tails(cst[:, 0:4], lext, 4)
                dve.wait_ge(s["lg"], 8)
                link(mul(lb[:], lb[:], lu[:]))
                dve.wait_ge(s["at_ok"], 1)
                link(mul(lh[:], la[:], la[:]))
                stt(out=lt[:], in0=lh[:], scalar=1.0, in1=lt[:], op0=ALU.add, op1=ALU.mult).then_inc(s["lt_ok"], 1)
                dve.wait_ge(s["lq_ok"], 1)
                link(mul(lb[:], lb[:], lt[:]))
                first = slice(SEQ, T, DEC_SEQ)
                link(mul(lt[:, :, 0:DEC_BATCH], la[:, :, first], h0[:]))
                link(add(lb[:, :, first], lb[:, :, first], lt[:, :, 0:DEC_BATCH]))
                V.memset(la[:, :, first], 0.0)
                link(V.memset(la[:, :, 0:1], 0.0))
                link(V.tensor_tensor_scan(lh.rearrange("p c t -> p (c t)"), la.rearrange("p c t -> p (c t)"),
                                          lb.rearrange("p c t -> p (c t)"), 0.0, ALU.mult, ALU.add))
                dve.wait_ge(s["pa"], 4)
                mul(zs[:, 0:4], zs[:, 0:4], lh[:]).then_inc(s["lru_ok"], 1)
                V.tensor_copy(lst[:, :, 0:1], lh[:, :, SEQ - 1:SEQ])
                V.tensor_copy(lst[:, :, 1:9], lh[:, :, SEQ + DEC_SEQ - 1:T:DEC_SEQ]).then_inc(s["lc_ok"], 1)
                for i in range(12, NP_NSA):
                    take(i)
                dve.wait_ge(s["gt_t"], 1)
                V.tensor_copy(gtok[:, 0:4, :], PS[:, 4, 0:4 * NSM].rearrange("p (k n) -> p k n", k=4)).then_inc(s["gt_ok"], 1)
                V.tensor_copy(gtok[0:T_S, 4, :], PS[0:T_S, 4, 4 * NSM:5 * NSM]).then_inc(s["gt_ok"], 1)
                dve.wait_ge(s["lo_t"], 1)
                V.tensor_copy(rowl[0:27], bank4(6, P, 27)).then_inc(s["lo_ok"], 1)
                V.tensor_copy(rowh[0:9], bank4(7, P, 9)).then_inc(s["lo_ok"], 1)
                dve.wait_ge(s["rstd_ok"], 2)
                for n in range(7):
                    gain = prm("qn") if n < 4 else prm("kn", n - 4)
                    stt(out=qk7[:, n], in0=qk7[:, n], scalar=gain, in1=rs7[:, n], op0=ALU.mult, op1=ALU.mult)\
                        .then_inc(s["nq_y"], 1)
                for n in range(7):
                    dve.wait_ge(s["nq_sw"], n + 1)
                    mul(halves(rs7[:, n]), pair(4 + 2 * (n % 2)), halves(C("sin"))).then_inc(s["nq_r"], 1)
                    link(mul(qk7[:, n], qk7[:, n], C("cos")))
                    add(qk7[:, n], qk7[:, n], rs7[:, n]).then_inc(s["qk_ok"], 1)
                dve.wait_ge(s["qk_ok"], 7)
                link(V.memset(kcp[:], 0.0))
                for g in range(KV):
                    m = slice(g * HD, (g + 1) * HD)
                    link(V.tensor_reduce(kcp[m, g], qk7[m, 4, 0:SEQ].rearrange("p (n c) -> p n c", c=CMP), AX.X, ALU.add))
                link(V.tensor_scalar(kcp[:], kcp[:], 1.0 / CMP, None, ALU.mult))
                dve.wait_ge(s["vc_mm"], 1)
                dve.wait_ge(s["gs_ok"], 2)
                hm = C("hmask")
                for r in range(REP):
                    ins = mul(vcb.rearrange("p (r g d) -> p r g d", r=REP, g=KV)[:, r],
                              PS[:, 7, 0:P].rearrange("p (g d) -> p g d", g=KV), bc(hm[:, r * KV:(r + 1) * KV], HD))
                ins.then_inc(s["c_ok"], 1)

                def per_head(ap):
                    return ap.rearrange("p (h d) -> p h d", h=HEADS)

                def gate(qt, br):
                    return gtok[:, qt, br * HEADS:(br + 1) * HEADS].rearrange("p (g r) -> p r g", g=KV)

                rl, f, cm, cl = (sm8[:, i, :] for i in (3, 4, 5, 6))
                f2 = f.rearrange("p (r g) -> p r g", r=REP)
                rl2 = rl.rearrange("p (r g) -> p r g", r=REP)
                for qt in range(4):
                    q0 = qt * P
                    pc3 = pc.rearrange("p (h n) -> p h n", h=HEADS)
                    dve.wait_ge(s["c_s"], qt + 1)
                    if qt == 0:
                        dve.wait_ge(s["kt_e"], NTILE)
                    link(add(pc3, PS[:, 7, 0:P].rearrange("p (h n) -> p h n", h=HEADS), rep(C("cmask", NCB, k=qt), HEADS)))
                    link(V.tensor_reduce(cm, pc3, AX.X, ALU.max))
                    sub(pc3, pc3, bc(cm, NCB)).then_inc(s["c_m"], 1)

                    def finish(br):
                        dve.wait_ge(s["a_v"], 2 * HEADS * qt + HEADS * (br + 1))
                        link(V.reciprocal(rl, sm8[:, 1 + br, :]))
                        link(mul(f2, rl2, gate(qt, 1 + br)))
                        mul(per_head(otmp), per_head(PS[:, br, :]), bc(f, HD)).then_inc(s["a_o"], 1)
                        dve.wait_ge(s["a_o"], 2 * qt + br + 1)
                        link(add(otok, otok, otmp))

                    for i in range(2 * HEADS + 2):
                        u = 2 * HEADS * qt + i
                        if i < 2 * HEADS:
                            dve.wait_ge(s["a_s"], u + 1)
                            diag = PS[:, 4 + u % 2, q0:q0 + P]
                            link(add(diag, diag, C("causal")))
                            V.tensor_reduce(sm8[:, 0, u % 4:u % 4 + 1], PS[:, 4 + u % 2, 0:q0 + P], AX.X, ALU.max,
                                            negate=True).then_inc(s["a_m"], 1)
                        v = u - 2
                        if i >= 2 and v % 2 == 1:
                            dve.wait_ge(s["a_t"], v + 1)
                            if v >= 2:
                                dve.wait_ge(s["a_v"], v - 1)
                            V.tensor_copy(pTring[1][:, 0:q0 + P], PS[:, 3, 0:q0 + P]).then_inc(s["a_cd"], 1)
                        if i == 5:
                            dve.wait_ge(s["c_t"], qt + 1)
                            V.tensor_copy(pcT, PS[:, 7, P:2 * P]).then_inc(s["c_c"], 1)
                        if i == 8:
                            dve.wait_ge(s["c_e"], qt + 1)
                            link(V.tensor_reduce(cl, pc3, AX.X, ALU.add))
                            link(V.reciprocal(rl, cl))
                            link(stt(out=f2, in0=rl2, scalar=C("cvalid", 1, k=qt), in1=gate(qt, 0),
                                     op0=ALU.mult, op1=ALU.mult))
                            dve.wait_ge(s["c_pv"], qt + 1)
                            mul(per_head(otok), per_head(PS[:, 6, :]), bc(f, HD)).then_inc(s["c_o"], 1)
                            dve.wait_ge(s["c_o"], qt + 1)
                        if i == 13:
                            finish(0)
                    finish(1)
                    dve.sem_inc(s["o_sum"], 1)
                    dve.wait_ge(s["o_t"], qt + 1)
                    mul(zs[:, 4:8, q0:q0 + P], zs[:, 4:8, q0:q0 + P], bank4(6)).then_inc(s["z_o"], 1)

                dve.wait_ge(s["gq_t"], 1)
                g_all = gsel.rearrange("p (k n) -> p k n", k=4)
                link(mul(g_all, PS[:, 5, 256:256 + 4 * NG].rearrange("p (k n) -> p k n", k=4), rep(C("gmask"), 4)))
                sgt = spb[:, 5, 0:12]
                V.tensor_reduce(sgt, gsel.rearrange("p (a h) -> p a h", h=HEADS), AX.X, ALU.add).then_inc(s["qb_ok"], 1)
                dve.wait_ge(s["lo_out"], l * LO_OUT + 64)
                link(V.memset(qb[:], 0.0))
                link(V.memset(exn[:], 0.0))
                for g in range(KV):
                    m = slice(g * HD, (g + 1) * HD)
                    for r in range(REP):
                        at = g * REP * DEC_SEQ + r * DEC_SEQ
                        ins = V.tensor_copy(qb[m, :, at:at + DEC_SEQ],
                                            qk7[m, r, SEQ:T].rearrange("p (b t) -> p b t", t=DEC_SEQ))
                    ins.then_inc(s["qb_ok"], 1)
                stat = sm8
                for b in range(DEC_BATCH):
                    k2, b2 = b // 2, b % 2
                    if b:
                        dve.wait_ge(s["s_sc"], b)
                    dve.wait_ge(s["s_t2"], b + 1)
                    V.tensor_copy(KT[:, 512:1024], PS[:, 3, :]).then_inc(s["s_e2"], 1)
                    dve.wait_ge(s["s_t3"], b + 1)
                    V.tensor_copy(KW, PS[:, 6, :]).then_inc(s["s_e3"], 1)
                    dve.wait_ge(s["s_kt"], b + 1)
                    V.tensor_copy(kcT, PS[:, 7, 256:256 + NPB]).then_inc(s["s_ke"], 1)
                    if b2 == 0:
                        continue
                    dve.wait_ge(s["s_sc"], b + 1)
                    V.tensor_reduce(stat[:, 5, 0:1], PS[:, 5, P:P + NPB], AX.X, ALU.max, negate=True).then_inc(s["s_cm"], 1)
                    V.tensor_copy(sw[:, DEC_SEQ:512], PS[:, 4, DEC_SEQ:512])
                    add(sw[:, 0:DEC_SEQ], PS[:, 4, 0:DEC_SEQ], C("winm"))
                    dve.wait_ge(s["s_ce"], k2 + 1)
                    link(V.reciprocal(stat[:, 5, 2:3], stat[:, 5, 1:2]))
                    V.tensor_scalar(cp, cp, stat[:, 5, 2:3], None, ALU.mult).then_inc(s["s_cn"], 1)
                    link(add(sw[:, 512:576], PS[:, 5, T_S:2 * T_S], C("newm", T_S, k=k2)))
                    V.tensor_reduce(stat[:, 6, 0:1], sw, AX.X, ALU.max, negate=True).then_inc(s["s_wm"], 1)
                    dve.wait_ge(s["s_im"], k2 + 1)
                    link(V.tensor_reduce(eqb, PS[:, 7, 288:288 + NPB].rearrange("p (n c) -> p n c", c=2), AX.X, ALU.add))
                    link(V.tensor_reduce(stat[:, 7, 2:3], eqb[:, 1:NSEL], AX.X, ALU.min))
                    link(stt(out=exn[:, 1:NSEL], in0=eqb[:, 1:NSEL], scalar=stat[:, 7, 2:3], in1=C("blkno")[:, 1:NSEL],
                             op0=ALU.is_le, op1=ALU.mult))
                    link(V.tensor_reduce(stat[:, 7, 3:4], exn[:, 1:NSEL], AX.X, ALU.max))
                    link(V.tensor_scalar(exn[:, 1:NSEL], C("blkno")[:, 1:NSEL], stat[:, 7, 3:4], NEG,
                                         ALU.is_equal, ALU.mult))
                    for c in range(2):
                        add(ss[:, c * 512:(c + 1) * 512].rearrange("p (n c) -> p n c", c=SLC),
                            PS[:, c, :].rearrange("p (n c) -> p n c", c=SLC), bc(exn[:, 8 * c:8 * c + 8], SLC))
                    link(add(ss[:, 1024:1088], PS[:, 5, 0:T_S], C("newm", T_S, k=k2)))
                    V.tensor_reduce(stat[:, 7, 0:1], ss, AX.X, ALU.max, negate=True).then_inc(s["s_sm"], 1)
                    dve.wait_ge(s["s_wc"], k2 + 1)
                    V.tensor_copy(pT[:, 1024:1536], PS[:, 6, :]).then_inc(s["s_mw"], 1)
                    dve.wait_ge(s["s_tr"], 2 * k2 + 2)
                    V.tensor_copy(pT[:, 512:1024], PS[:, 3, :]).then_inc(s["s_tb"], 1)
                    for i, br in ((6, 2), (7, 1)):
                        link(V.reciprocal(stat[:, i, 4:5], stat[:, i, 1:2]))
                        link(mul(stat[:, i, 5:6], stat[:, i, 4:5], sgt[:, 3 * k2 + br:3 * k2 + br + 1]))
                    dve.wait_ge(s["s_pv"], 2 * k2 + 2)
                    link(V.tensor_scalar(orow, PS[:, 4, 0:P], stat[:, 7, 5:6], None, ALU.mult))
                    link(stt(out=orow, in0=PS[:, 4, P:2 * P], scalar=stat[:, 6, 5:6], in1=orow, op0=ALU.mult, op1=ALU.add))
                    stt(out=orow, in0=PS[:, 4, 2 * P:3 * P], scalar=sgt[:, 3 * k2:3 * k2 + 1], in1=orow,
                        op0=ALU.mult, op1=ALU.add).then_inc(s["s_or"], 1)
                    dve.wait_ge(s["s_ot"], k2 + 1)
                    for g in range(KV):
                        m = slice(g * HD, (g + 1) * HD)
                        at = SEQ + 2 * k2 * DEC_SEQ
                        z = zs[m, 4:8, at:at + 2 * DEC_SEQ].rearrange("p r (b t) -> p b r t", b=2)
                        o = PS[m, 5, 0:P].rearrange("p (b g r t) -> p b g r t", b=2, g=KV, r=REP)[:, :, g]
                        mul(z, z, o).then_inc(s["s_z"], 1)

                dve.wait_ge(s["s_z"], 8)
                dve.wait_ge(s["kv_out"], l * KV_OUT + KV_OUT)
                link(V.memset(dext[:, :, 0:HIST], 0.0))
                dve.wait_ge(s["dh_t"], 1)
                for c in range(12):
                    ins = V.tensor_copy(dext[:, c, HIST + SEQ:EXT].rearrange("p (b t) -> p b t", t=S_EXT)[:, :, 0:HIST],
                                        PS[:, 4, c * 24:(c + 1) * 24].rearrange("p (b t) -> p b t", t=HIST))
                ins.then_inc(s["dh_c"], 1)
                dve.wait_ge(s["dh_c"], 1)
                for c in range(12):
                    i = NP_NSA + c
                    take(i)
                    dve.wait_ge(s["pa"] if PROJ[i][2] == "A" else s["pv"], taken(i + 1, PROJ[i][2]))
                    conv(dc[:, c], dext[:, c], lambda j: prm("dconv", 12 * j + c), None, s["conv_ok"])
                tails(cst[:, 4:16], dext, 12).then_inc(s["dc_ok"], 1)
                x = spb[:, 5, :].rearrange("p (k h) -> p k h", h=DN_H)
                dve.wait_ge(s["small_in"], 8 * 16)
                link(add(x, gtok[:, :, NG:NG + DN_H], rep(dnp[:, DN_H:2 * DN_H], NTILE)))
                stt(out=spb[:, 0, :], in0=spb[:, 5, :], scalar=-1.0, in1=spb[:, 5, :], op0=ALU.mult, op1=ALU.max).then_inc(s["sp_abs"], 1)
                dve.wait_ge(s["lo_t"], 2)
                V.tensor_copy(rowd, PS[0:27, 5:8, :].rearrange("p b n -> p (b n)")).then_inc(s["lo_ok"], 1)
                dve.wait_ge(s["sp_exp"], 3)
                softplus_tail(20)
                stt(out=g4[:], in0=spb[:, 4, :].rearrange("p (k h) -> p k h", h=DN_H), scalar=-1.0,
                    in1=rep(dnp[:, 0:DN_H], NTILE), op0=ALU.mult, op1=ALU.mult).then_inc(s["gb_ok"], 1)
                dve.wait_ge(s["rstd_ok"], 3)
                for n in range(8):
                    stt(out=dc[:, n], in0=dc[:, n], scalar=DN_D ** -0.5 if n < 4 else 1.0, in1=dsq[:, n],
                        op0=ALU.mult, op1=ALU.mult).then_inc(s["n_ok"], 1)
                dve.wait_ge(s["n_ok"], 8)
                dve.wait_ge(s["silu_ok"], 12)
                link(V.memset(Sp[:], 0.0))
                n_iw = n_ix = n_f = 0
                for group in DN_GROUPS:
                    for li, k in enumerate(group):
                        t, n = TILES[k]
                        sfx = "" if t < SEQ else "s"
                        eG, eR, gc, ekb = sm8[0:n, 9, 0:4], sm8[0:n, 9, 4:8], sm8[0:n, 10, 0:4], sm8[0:n, 11, 0:4]
                        beta = gtok[0:n, k, NG + DN_H:NSM]
                        D = tmp["W"][0:n, li, :, 0:n]
                        dve.wait_ge(s["p_e"], k + 1)
                        link(V.tensor_copy(gc, PS[0:n, 6, 0:DN_H]))
                        for h in range(DN_H):
                            ins = V.tensor_scalar(D[:, h], PS[0:n, 0, h * P:h * P + n], gc[:, h:h + 1], 0.0,
                                                  ALU.subtract, ALU.min)
                        ins.then_inc(s["p_x"], 1)
                        link(mul(ekb, beta, eG))
                        dve.wait_ge(s["p_g"], 3 * k + 3)
                        mul(tmp["kb"][0:n, li], bank4(4, P, n), bc(ekb, P)).then_inc(s["p_k"], 1)
                        mul(grp["kd"][0:n, li], bank4(4, P, n), bc(eR, P)).then_inc(s["p_k"], 1)
                        mul(tmp["bv"][0:n, li], bank4(5, P, n), bc(beta, P)).then_inc(s["p_k"], 1)
                        mul(dc[:, 0:4, t:t + n], dc[:, 0:4, t:t + n], tmp["E"][:, li, :, 0:n])
                        dve.wait_ge(s["p_d"], k + 1)
                        B, Q = tmp["B"][0:n, li, :, 0:n], grp["qk"][0:n, li, :, 0:n]
                        link(mul(D, D, rep(C("U" + sfx, P)[0:n, 0:n], DN_H)))
                        link(mul(B, bank4(2, n, n), D))
                        mul(Q, bank4(3, n, n), D)
                        link(mul(B, bank4(1, n, n), B))
                        mul(B, B, rep(C("SU" + sfx, P)[0:n, 0:n], DN_H)).then_inc(s["p_b"], 1)
                    levels = 6 if TILES[group[0]][0] < SEQ else 3
                    for lev in range(levels):
                        for li, k in enumerate(group):
                            n = TILES[k][1]
                            n_iw += 1
                            dve.wait_ge(s["i_w"], n_iw)
                            mul(tmp["W"][0:n, li, :, 0:n], bank4(li, n, n), rep(C("lev", P, k=lev)[0:n, 0:n], DN_H))\
                                .then_inc(s["i_wm"], 1)
                        for li, k in enumerate(group):
                            n = TILES[k][1]
                            n_ix += 1
                            X, Y, W = (tmp[a][0:n, li, :, 0:n] for a in "XYW")
                            I = rep(ident[0:n, 0:n], DN_H)
                            dve.wait_ge(s["i_x"], n_ix)
                            if lev < levels - 1:
                                link(sub(X, I if lev == 0 else X, W if lev == 0 else bank4(2 + li, n, n)))
                            sub(Y, I if lev == 0 else Y, bank4(4 + li, n, n)).then_inc(s["i_xm"], 1)
                    for li, k in enumerate(group):
                        t, n = TILES[k]
                        n_f += 1
                        dve.wait_ge(s["f_mm"], n_f)
                        if t < SEQ:
                            V.tensor_copy(grp["u"][0:n, li], bank4(6, P, n)).then_inc(s["f_u"], 1)
                        else:
                            V.tensor_copy(tmp["X"][:, 0, :, 0:n], bank4(6, n)).then_inc(s["f_u"], 1)
                    if TILES[group[0]][0] >= SEQ:
                        break
                    for li, k in enumerate(group):
                        for half in range(2):
                            c = 2 * k + half
                            rw = slice(half * CHUNK, (half + 1) * CHUNK)
                            dve.wait_ge(s["q_w"], c + 1)
                            if li == 0 and half == 0:
                                dve.wait_ge(s["f_u"], n_f)
                            sub(grp["u"][rw, li], grp["u"][rw, li], bank4(0)[rw]).then_inc(s["q_v"], 1)
                            dve.wait_ge(s["q_s"], c + 1)
                            for h in range(DN_H):
                                last = tmp["E"][:, li, h, rw.stop - 1:rw.stop]
                                ins = stt(out=Sp[:, h], in0=Sp[:, h], scalar=last, in1=PS[:, 2, h * P:(h + 1) * P],
                                          op0=ALU.mult, op1=ALU.add)
                            ins.then_inc(s["q_n"], 1)
                dve.wait_ge(s["f_u"], n_f)
                dve.wait_ge(s["b_ws"], 1)
                sub(tmp["W"][:, 0, :, 0:T_S], tmp["X"][:, 0, :, 0:T_S],
                    PS[:, 0, 0:DN_H * T_S].rearrange("p (h n) -> p h n", h=DN_H)).then_inc(s["b_vt"], 1)
                dve.wait_ge(s["b_tr"], 1)
                V.tensor_copy(grp["u"][0:T_S, 0], bank4(2, P, T_S)).then_inc(s["b_vn"], 1)
                dve.wait_ge(s["b_vn"], 1)
                for h in range(DN_H + 1):
                    if h < DN_H:
                        if h >= 2:
                            dve.wait_ge(s["b_sm"], h - 1)
                        mul(bvm[h % 2][0:T_S].rearrange("p (b e) -> p b e", b=DEC_BATCH),
                            rep(grp["u"][0:T_S, 0, h, :], DEC_BATCH), bc(C("bmask")[0:T_S], P)).then_inc(s["b_vm"], 1)
                    if h >= 1:
                        g = h - 1
                        last = tmp["E"][:, 0, g, DEC_SEQ - 1:T_S:DEC_SEQ]
                        if g == 0:
                            dve.wait_ge(s["b_o"], 1)
                        link(mul(S0[:, :, g], S0[:, :, g], bc(last, P)))
                        dve.wait_ge(s["b_sm"], h)
                        add(S0[:, :, g], S0[:, :, g],
                            PS[:, 4 + 2 * (g % 2):6 + 2 * (g % 2), :].rearrange("p a (b e) -> p (a b) e", e=P))\
                            .then_inc(s["b_sn"], 1)
                dve.wait_ge(s["rstd_ok"], 4)
                for n in range(DN_H):
                    link(stt(out=dc[:, n], in0=dc[:, n], scalar=prm("on"), in1=dc[:, 4 + n], op0=ALU.mult, op1=ALU.mult))
                mul(zs[:, 8:12], zs[:, 8:12], dc[:, 0:4]).then_inc(s["dn_ok"], 1)
                dve.wait_ge(s["b_out"], l * 16 + 16)
                for c in range(24):
                    br, j = c % 6 // 2, 2 * (c // 6) + c % 2
                    dve.wait_ge(s["pa"], taken(NP_DN + c + 1, "A"))
                    dve.wait_ge(s["po"], c + 1)
                    dst = mT[:, j] if br == 0 else mpr
                    mul(halves(dst), halves(sg[:, c % 2]), pair(4 + 2 * (c % 2))).then_inc(s["mp"], 1)
                    if br:
                        dve.wait_ge(s["mp"], c + 1)
                        ins = add(mT[:, j], mT[:, j], mpr)
                        if br == NBR - 1:
                            ins.then_inc(s["mg_ok"], 1)
                            dve.wait_ge(s["mg_ok"], j + 1)
                        else:
                            link(ins)
                for i in range(NP_MG, len(PROJ)):
                    take(i)
                dve.wait_ge(s["pv"], taken(len(PROJ), "V"))
                dve.sem_inc(s["done"], 1)
                dve.wait_ge(s["go"], l + 1)
            for k, (t, n) in enumerate(TILES):
                for h in range(2):
                    u = 2 * k + h
                    dve.wait_ge(s["y_t"], u + 1)
                    V.tensor_copy(arena[0:n, k * D_MODEL + h * 512:k * D_MODEL + (h + 1) * 512],
                                  PS[0:n, u % 4, :]).then_inc(s["y_e"], 1)


_INS = ["x_prompt", "x_sample", "cache_nsa_kv", "page_table", "state_nsa_win", "state_lru_h", "state_lru_conv",
        "state_dn_S", "state_dn_conv", "norm_gain", "w_in", "lru_conv_w", "lru_conv_b", "lru_wa", "lru_ba",
        "lru_wx", "lru_bx", "lru_lambda", "nsa_q_norm", "nsa_k_norm", "dn_conv_w", "dn_A_log", "dn_dt_bias",
        "dn_o_norm", "w_lru_out", "w_nsa_out", "w_dn_out", "w_out"]
_OUTS = [
    ("y_prompt", (1, SEQ, D_MODEL)), ("y_sample", (DEC_BATCH, DEC_SEQ, D_MODEL)),
    ("kv_prompt", (DEPTH, 1, SEQ, 4, KV, HD)), ("kv_sample", (DEPTH, DEC_BATCH, DEC_SEQ, 4, KV, HD)),
    ("win_prompt", (DEPTH, 1, WINDOW, 2, KV, HD)), ("win_sample", (DEPTH, DEC_BATCH, WINDOW, 2, KV, HD)),
    ("lru_h_prompt", (DEPTH, 1, D_RNN)), ("lru_h_sample", (DEPTH, DEC_BATCH, D_RNN)),
    ("lru_conv_prompt", (DEPTH, 1, HIST, D_RNN)), ("lru_conv_sample", (DEPTH, DEC_BATCH, HIST, D_RNN)),
    ("dn_S_prompt", (DEPTH, 1, DN_H, DN_D, DN_D)), ("dn_S_sample", (DEPTH, DEC_BATCH, DN_H, DN_D, DN_D)),
    ("dn_conv_prompt", (DEPTH, 1, HIST, 3 * DN_W)), ("dn_conv_sample", (DEPTH, DEC_BATCH, HIST, 3 * DN_W)),
]


def kernel(**inputs):
    import concourse.bacc as _bacc
    from concourse.bass_utils import run_bass_kernel_spmd as _run

    nc = _bacc.Bacc("TRN2", target_bir_lowering=False, num_devices=1)
    arrays, dram, out = {"in_con": constants()}, {}, {}
    for name in _INS:
        arrays["in_" + name] = np.ascontiguousarray(inputs[name])
    for key, a in arrays.items():
        dram[key[3:]] = nc.dram_tensor(key, a.shape, mybir.dt.from_np(a.dtype), kind="ExternalInput").ap()
    for name, shape in _OUTS:
        out[name] = nc.dram_tensor("out_" + name, shape, F32, kind="ExternalOutput").ap()
    hybrid_trunk(nc, dram, out)
    r = _run(nc, [arrays], core_ids=[0])
    return tuple(r.results[0]["out_" + name] for name, _ in _OUTS)
```
